# Optimizing a Trainium2 kernel written in Bass

```python
import math
import jax
import jax.numpy as jnp
from jax import lax
import numpy as np
import jax, jax.numpy as jnp

D_MODEL = 1024
BATCH = 1
SEQ = 256
DEPTH = 2

BLOCK_Q = 128
EPS = 1e-6
NEG = -1e30
D_FF = 2816

MLA_HEADS = 8
MLA_Q_RANK = 256
MLA_KV_RANK = 128
MLA_NOPE = 64
MLA_ROPE = 32
MLA_V = 64
ROPE_THETA = 10000.0

SWA_HEADS = 8
SWA_KV_HEADS = 2
SWA_HD = 64
SWA_WINDOW = 128

NSA_HEADS = 8
NSA_KV_HEADS = 2
NSA_HD = 64
NSA_CMP_LEN = 32
NSA_CMP_STRIDE = 16
NSA_CMP_HIDDEN = 128
NSA_SEL_LEN = 64
NSA_TOPK = 16
NSA_WINDOW = 512
NSA_FORCE = 1e4

DIFF_HEADS = 4
DIFF_HD = 64

N_BUCKETS = 32
MAX_DIST = 128
N_BIAS_HEADS = SWA_HEADS + NSA_HEADS + DIFF_HEADS

N_BRANCH = 4
BRANCH_W = 512

COL_SIZES = (
    MLA_Q_RANK, MLA_KV_RANK, MLA_ROPE,
    SWA_HEADS * SWA_HD, SWA_KV_HEADS * SWA_HD, SWA_KV_HEADS * SWA_HD,
    NSA_HEADS * NSA_HD,
    NSA_KV_HEADS * NSA_HD, NSA_KV_HEADS * NSA_HD,
    NSA_KV_HEADS * NSA_HD, NSA_KV_HEADS * NSA_HD,
    NSA_KV_HEADS * NSA_HD, NSA_KV_HEADS * NSA_HD,
    3 * NSA_HEADS,
    DIFF_HEADS * 2 * DIFF_HD, DIFF_HEADS * 2 * DIFF_HD, DIFF_HEADS * 2 * DIFF_HD,
)
IN_COLS = sum(COL_SIZES)


def rmsnorm(x, g):
    xf = x.astype(jnp.float32)
    y = xf * lax.rsqrt(jnp.mean(xf * xf, -1, keepdims=True) + EPS)
    return (y * g.astype(jnp.float32)).astype(x.dtype)

def swiglu(x, w_gate, w_up, w_down):
    return (jax.nn.silu(x @ w_gate) * (x @ w_up)) @ w_down

def rope(x, pos):
    half = x.shape[-1] // 2
    freqs = ROPE_THETA ** (-jnp.arange(half, dtype=jnp.float32) / half)
    ang = pos[:, None].astype(jnp.float32) * freqs
    cos, sin = jnp.cos(ang), jnp.sin(ang)
    xf = x.astype(jnp.float32)
    x1, x2 = xf[..., :half], xf[..., half:]
    return jnp.concatenate([x1 * cos - x2 * sin, x1 * sin + x2 * cos], -1).astype(x.dtype)

def t5_bucket(dist):
    n = jnp.maximum(dist, 0)
    max_exact = N_BUCKETS // 2
    nf = jnp.maximum(n, 1).astype(jnp.float32)
    large = max_exact + (jnp.log(nf / max_exact) / math.log(MAX_DIST / max_exact)
                         * (N_BUCKETS - max_exact)).astype(jnp.int32)
    large = jnp.minimum(large, N_BUCKETS - 1)
    return jnp.where(n < max_exact, n, large)

def rel_bias(table, q_pos, k_pos):
    b = t5_bucket(q_pos[:, None] - k_pos[None, :])
    return jnp.moveaxis(table[b], -1, 0).astype(jnp.float32)

def masked_softmax(s, mask):
    s = jnp.where(mask, s, NEG)
    m = jnp.max(s, -1, keepdims=True)
    e = jnp.where(mask, jnp.exp(s - m), 0.0)
    den = jnp.sum(e, -1, keepdims=True)
    return e / jnp.where(den > 0, den, 1.0)

def dense_causal_attn(q, k, v, scale):
    B, H, S, _ = q.shape
    dv = v.shape[-1]
    kpos = jnp.arange(S)

    def blk(i):
        start = i * BLOCK_Q
        qpos = start + jnp.arange(BLOCK_Q)
        qb = lax.dynamic_slice_in_dim(q, start, BLOCK_Q, axis=2)
        s = jnp.einsum('bhqd,bhkd->bhqk', qb, k).astype(jnp.float32) * scale
        s = jnp.where(kpos[None, :] <= qpos[:, None], s, NEG)
        p = jax.nn.softmax(s, -1)
        return jnp.einsum('bhqk,bhkd->bhqd', p.astype(v.dtype), v)

    o = lax.map(blk, jnp.arange(S // BLOCK_Q))
    return o.transpose(1, 0, 3, 2, 4).reshape(B, S, H * dv)

def banded_attn(q, k, v, window, table, sinks):
    B, Hkv, G, S, d = q.shape
    dv = v.shape[-1]
    nprev = -(-window // BLOCK_Q)
    pad = nprev * BLOCK_Q
    span = pad + BLOCK_Q
    kp = jnp.pad(k, ((0, 0), (0, 0), (pad, 0), (0, 0)))
    vp = jnp.pad(v, ((0, 0), (0, 0), (pad, 0), (0, 0)))
    scale = d ** -0.5

    def blk(i):
        start = i * BLOCK_Q
        qpos = start + jnp.arange(BLOCK_Q)
        kpos = start - pad + jnp.arange(span)
        qb = lax.dynamic_slice_in_dim(q, start, BLOCK_Q, axis=3)
        kb = lax.dynamic_slice_in_dim(kp, start, span, axis=2)
        vb = lax.dynamic_slice_in_dim(vp, start, span, axis=2)
        s = jnp.einsum('bhgqd,bhkd->bhgqk', qb, kb).astype(jnp.float32) * scale
        s = s + rel_bias(table, qpos, kpos).reshape(Hkv, G, BLOCK_Q, span)
        dist = qpos[:, None] - kpos[None, :]
        mask = (dist >= 0) & (dist < window) & (kpos[None, :] >= 0)
        s = jnp.where(mask, s, NEG)
        if sinks is None:
            p = jax.nn.softmax(s, -1)
        else:
            sk = sinks.astype(jnp.float32).reshape(Hkv, G, 1, 1)
            m = jnp.maximum(jnp.max(s, -1, keepdims=True), sk)
            e = jnp.exp(s - m)
            p = e / (jnp.sum(e, -1, keepdims=True) + jnp.exp(sk - m))
        return jnp.einsum('bhgqk,bhkd->bhgqd', p.astype(vb.dtype), vb)

    o = lax.map(blk, jnp.arange(S // BLOCK_Q))
    return jnp.moveaxis(o, 0, 3).reshape(B, Hkv, G, S, dv)

def mla_mixer(cq, ckv, k_rope, q_norm, kv_norm, w_uq, w_ukv, pos):
    B, S, _ = cq.shape
    H = MLA_HEADS
    q = (rmsnorm(cq, q_norm) @ w_uq).reshape(B, S, H, MLA_NOPE + MLA_ROPE).transpose(0, 2, 1, 3)
    q = jnp.concatenate([q[..., :MLA_NOPE], rope(q[..., MLA_NOPE:], pos)], -1)
    kv = (rmsnorm(ckv, kv_norm) @ w_ukv).reshape(B, S, H, MLA_NOPE + MLA_V).transpose(0, 2, 1, 3)
    k_r = jnp.broadcast_to(rope(k_rope[:, None], pos), (B, H, S, MLA_ROPE))
    k = jnp.concatenate([kv[..., :MLA_NOPE], k_r], -1)
    v = kv[..., MLA_NOPE:]
    return dense_causal_attn(q, k, v, (MLA_NOPE + MLA_ROPE) ** -0.5)

def swa_mixer(q, k, v, sinks, table):
    B, S, _ = q.shape
    G = SWA_HEADS // SWA_KV_HEADS
    q = q.reshape(B, S, SWA_KV_HEADS, G, SWA_HD).transpose(0, 2, 3, 1, 4)
    k = k.reshape(B, S, SWA_KV_HEADS, SWA_HD).transpose(0, 2, 1, 3)
    v = v.reshape(B, S, SWA_KV_HEADS, SWA_HD).transpose(0, 2, 1, 3)
    o = banded_attn(q, k, v, SWA_WINDOW, table, sinks)
    return o.transpose(0, 3, 1, 2, 4).reshape(B, S, SWA_HEADS * SWA_HD)

def nsa_compress(t, pos_emb, w1, w2):
    B, Hkv, S, d = t.shape
    nc = (S - NSA_CMP_LEN) // NSA_CMP_STRIDE + 1
    idx = np.arange(nc)[:, None] * NSA_CMP_STRIDE + np.arange(NSA_CMP_LEN)[None, :]
    blocks = jnp.take(t, jnp.asarray(idx, dtype=jnp.int32), axis=2) + pos_emb
    hdn = jax.nn.gelu(blocks.reshape(B, Hkv, nc, NSA_CMP_LEN * d) @ w1)
    return hdn @ w2

def nsa_mixer(q, kc, vc, ks, vs, kw, vw, gate_logits, cmp_pos, cmp_w1, cmp_w2, table):
    B, S, _ = q.shape
    Hkv, G, d = NSA_KV_HEADS, NSA_HEADS // NSA_KV_HEADS, NSA_HD
    SEL = NSA_SEL_LEN
    q = q.reshape(B, S, Hkv, G, d).transpose(0, 2, 3, 1, 4)

    def heads(t):
        return t.reshape(B, S, Hkv, d).transpose(0, 2, 1, 3)

    kc, vc, ks, vs, kw, vw = heads(kc), heads(vc), heads(ks), heads(vs), heads(kw), heads(vw)
    scale = d ** -0.5
    kcmp = nsa_compress(kc, cmp_pos[0], cmp_w1[0], cmp_w2[0])
    vcmp = nsa_compress(vc, cmp_pos[1], cmp_w1[1], cmp_w2[1])
    nc = kcmp.shape[2]
    c_start = np.arange(nc) * NSA_CMP_STRIDE
    c_last = jnp.asarray(c_start + NSA_CMP_LEN - 1, dtype=jnp.int32)
    nsel = S // SEL
    s_start = np.arange(nsel) * SEL
    overlap = jnp.asarray(((c_start[:, None] < s_start[None, :] + SEL)
                           & (s_start[None, :] < c_start[:, None] + NSA_CMP_LEN)).astype(np.float32))
    topk = min(NSA_TOPK, nsel)
    ksb = ks.reshape(B, Hkv, nsel, SEL, d)
    vsb = vs.reshape(B, Hkv, nsel, SEL, d)
    tab = table.reshape(N_BUCKETS, Hkv, G)
    gather = jax.vmap(jax.vmap(lambda blocks, ix: blocks[ix]))
    group_bias = jax.vmap(lambda bk, tb: tb[bk], in_axes=(1, 1), out_axes=1)
    sel_ids = jnp.arange(nsel)

    def blk(i):
        start = i * BLOCK_Q
        qpos = start + jnp.arange(BLOCK_Q)
        qb = lax.dynamic_slice_in_dim(q, start, BLOCK_Q, axis=3)
        s_c = jnp.einsum('bhgqd,bhcd->bhgqc', qb, kcmp).astype(jnp.float32) * scale
        p_c = masked_softmax(s_c, c_last[None, :] <= qpos[:, None])
        o_c = jnp.einsum('bhgqc,bhcd->bhgqd', p_c.astype(vcmp.dtype), vcmp)
        imp = jnp.einsum('bhgqc,cn->bhqn', p_c, overlap)
        cur = qpos // SEL
        causal = sel_ids[None, :] * SEL <= qpos[:, None]
        forced = ((sel_ids[None, :] == 0) | (sel_ids[None, :] == cur[:, None])
                  | (sel_ids[None, :] == cur[:, None] - 1))
        imp = jnp.where(causal, jnp.where(forced, NSA_FORCE, imp), -1.0)
        _, top = lax.top_k(imp, topk)
        k_sel = gather(ksb, top).reshape(B, Hkv, BLOCK_Q, topk * SEL, d)
        v_sel = gather(vsb, top).reshape(B, Hkv, BLOCK_Q, topk * SEL, d)
        kpos = (top[..., None] * SEL + jnp.arange(SEL)).reshape(B, Hkv, BLOCK_Q, topk * SEL)
        dist = qpos[:, None] - kpos
        bias = jnp.moveaxis(group_bias(t5_bucket(dist), tab), -1, 2).astype(jnp.float32)
        s_s = jnp.einsum('bhgqd,bhqkd->bhgqk', qb, k_sel).astype(jnp.float32) * scale + bias
        s_s = jnp.where((dist >= 0)[:, :, None], s_s, NEG)
        p_s = jax.nn.softmax(s_s, -1)
        o_s = jnp.einsum('bhgqk,bhqkd->bhgqd', p_s.astype(v_sel.dtype), v_sel)
        return o_c, o_s

    o_c, o_s = lax.map(blk, jnp.arange(S // BLOCK_Q))
    o_c = jnp.moveaxis(o_c, 0, 3).reshape(B, Hkv, G, S, d)
    o_s = jnp.moveaxis(o_s, 0, 3).reshape(B, Hkv, G, S, d)
    o_w = banded_attn(q, kw, vw, NSA_WINDOW, table, None)
    g = jax.nn.sigmoid(gate_logits.astype(jnp.float32)).reshape(B, S, Hkv, G, 3).transpose(0, 2, 3, 1, 4)
    o = g[..., 0:1] * o_c + g[..., 1:2] * o_s + g[..., 2:3] * o_w
    return o.astype(q.dtype).transpose(0, 3, 1, 2, 4).reshape(B, S, NSA_HEADS * d)

def diff_mixer(q, k, v, lam_params, subln, table, layer):
    B, S, _ = q.shape
    H, d = DIFF_HEADS, DIFF_HD
    q = q.reshape(B, S, H, 2, d).transpose(0, 2, 3, 1, 4)
    k = k.reshape(B, S, H, 2, d).transpose(0, 2, 3, 1, 4)
    v = v.reshape(B, S, H, 2 * d).transpose(0, 2, 1, 3)
    lam_init = 0.8 - 0.6 * math.exp(-0.3 * layer)
    lp = lam_params.astype(jnp.float32)
    lam = jnp.exp(jnp.sum(lp[0] * lp[1])) - jnp.exp(jnp.sum(lp[2] * lp[3])) + lam_init
    scale = d ** -0.5
    kpos = jnp.arange(S)

    def blk(i):
        start = i * BLOCK_Q
        qpos = start + jnp.arange(BLOCK_Q)
        qb = lax.dynamic_slice_in_dim(q, start, BLOCK_Q, axis=3)
        s = jnp.einsum('bhmqd,bhmkd->bhmqk', qb, k).astype(jnp.float32) * scale
        s = s + rel_bias(table, qpos, kpos)[:, None]
        s = jnp.where(kpos[None, :] <= qpos[:, None], s, NEG)
        p = jax.nn.softmax(s, -1)
        a = p[:, :, 0] - lam * p[:, :, 1]
        return jnp.einsum('bhqk,bhkd->bhqd', a.astype(v.dtype), v)

    o = lax.map(blk, jnp.arange(S // BLOCK_Q))
    o = jnp.moveaxis(o, 0, 2).reshape(B, H, S, 2 * d)
    o = rmsnorm(o, subln) * (1.0 - lam_init)
    return o.transpose(0, 2, 1, 3).reshape(B, S, H * 2 * d)

def first_inputs(seed: int = 0) -> dict:
    key = jax.random.key(seed)
    k = jax.random.split(key, 22)
    f32 = jnp.float32

    def w(kk, shape, fan_in):
        return jax.random.normal(kk, shape, f32) * (fan_in ** -0.5)

    def gain(kk, shape):
        return 1.0 + 0.05 * jax.random.normal(kk, shape, f32)

    L, d = NSA_CMP_LEN, NSA_HD
    return {
        'x': jax.random.normal(k[0], (BATCH, SEQ, D_MODEL), f32),
        'norm_g': gain(k[1], (DEPTH, 3, D_MODEL)),
        'w_in': w(k[2], (DEPTH, D_MODEL, IN_COLS), D_MODEL),
        'mla_q_norm': gain(k[3], (DEPTH, MLA_Q_RANK)),
        'mla_kv_norm': gain(k[4], (DEPTH, MLA_KV_RANK)),
        'mla_w_uq': w(k[5], (DEPTH, MLA_Q_RANK, MLA_HEADS * (MLA_NOPE + MLA_ROPE)), MLA_Q_RANK),
        'mla_w_ukv': w(k[6], (DEPTH, MLA_KV_RANK, MLA_HEADS * (MLA_NOPE + MLA_V)), MLA_KV_RANK),
        'swa_sinks': 0.5 * jax.random.normal(k[7], (DEPTH, SWA_HEADS), f32),
        'nsa_cmp_pos': 0.1 * jax.random.normal(k[8], (DEPTH, 2, L, d), f32),
        'nsa_cmp_w1': w(k[9], (DEPTH, 2, L * d, NSA_CMP_HIDDEN), L * d),
        'nsa_cmp_w2': w(k[10], (DEPTH, 2, NSA_CMP_HIDDEN, d), NSA_CMP_HIDDEN),
        'diff_lambda': 0.1 * jax.random.normal(k[11], (DEPTH, 4, DIFF_HD), f32),
        'diff_subln': gain(k[12], (DEPTH, 2 * DIFF_HD)),
        'rel_bias_table': 0.2 * jax.random.normal(k[13], (N_BUCKETS, N_BIAS_HEADS), f32),
        'w_branch': w(k[14], (DEPTH, N_BRANCH, BRANCH_W, D_MODEL), BRANCH_W),
        'w_gate': w(k[15], (DEPTH, N_BRANCH, D_MODEL, D_MODEL), D_MODEL),
        'w_o': w(k[16], (DEPTH, D_MODEL, D_MODEL), D_MODEL),
        'ffn_w_gate': w(k[17], (DEPTH, 2, D_MODEL, D_FF), D_MODEL),
        'ffn_w_up': w(k[18], (DEPTH, 2, D_MODEL, D_FF), D_MODEL),
        'ffn_w_down': w(k[19], (DEPTH, 2, D_FF, D_MODEL), D_FF),
        'final_g': gain(k[20], (D_MODEL,)),
    }

def first_block(x, norm_g, w_in, mla_q_norm, mla_kv_norm, mla_w_uq, mla_w_ukv, swa_sinks,
              nsa_cmp_pos, nsa_cmp_w1, nsa_cmp_w2, diff_lambda, diff_subln, rel_bias_table,
              w_branch, w_gate, w_o, ffn_w_gate, ffn_w_up, ffn_w_down, final_g):
    S = x.shape[1]
    pos = jnp.arange(S, dtype=jnp.int32)
    tab_swa = rel_bias_table[:, :SWA_HEADS]
    tab_nsa = rel_bias_table[:, SWA_HEADS:SWA_HEADS + NSA_HEADS]
    tab_diff = rel_bias_table[:, SWA_HEADS + NSA_HEADS:]
    offs = [int(o) for o in np.cumsum(COL_SIZES)[:-1]]
    h = x
    for l in range(DEPTH):
        h = h + 0.5 * swiglu(rmsnorm(h, norm_g[l, 0]), ffn_w_gate[l, 0], ffn_w_up[l, 0], ffn_w_down[l, 0])
        u = rmsnorm(h, norm_g[l, 1])
        cols = u @ w_in[l]
        (cq, ckv, krope, sq, sk, sv, nq, nkc, nvc, nks, nvs, nkw, nvw, ngate,
         dq, dk, dv) = jnp.split(cols, offs, axis=-1)
        y_a = mla_mixer(cq, ckv, krope, mla_q_norm[l], mla_kv_norm[l], mla_w_uq[l], mla_w_ukv[l], pos)
        y_b = swa_mixer(sq, sk, sv, swa_sinks[l], tab_swa)
        y_c = nsa_mixer(nq, nkc, nvc, nks, nvs, nkw, nvw, ngate,
                        nsa_cmp_pos[l], nsa_cmp_w1[l], nsa_cmp_w2[l], tab_nsa)
        y_d = diff_mixer(dq, dk, dv, diff_lambda[l], diff_subln[l], tab_diff, l)
        merged = jax.nn.sigmoid(u @ w_gate[l, 0]) * (y_a @ w_branch[l, 0])
        merged = merged + jax.nn.sigmoid(u @ w_gate[l, 1]) * (y_b @ w_branch[l, 1])
        merged = merged + jax.nn.sigmoid(u @ w_gate[l, 2]) * (y_c @ w_branch[l, 2])
        merged = merged + jax.nn.sigmoid(u @ w_gate[l, 3]) * (y_d @ w_branch[l, 3])
        h = h + merged @ w_o[l]
        h = h + 0.5 * swiglu(rmsnorm(h, norm_g[l, 2]), ffn_w_gate[l, 1], ffn_w_up[l, 1], ffn_w_down[l, 1])
    return rmsnorm(h, final_g)


N_MIXERS = 2
N_ATTN_LAYERS = (DEPTH + 1) // 2
N_RET_LAYERS = DEPTH // 2
NORM_EPS = 1e-6
N_NORMS = 6


DILATED_GROUPS = ((128, 1), (512, 4), (2048, 16))
N_GROUPS = len(DILATED_GROUPS)
H_A = 16
DH_A = 64
D_A = H_A * DH_A
ATTN_IN_COLS = N_GROUPS * 3 * D_A
BLK = 64
NEG_INF = -1e30

NUM_BUCKETS = 32
REL_MAX_DISTANCE = 1024

H_R = 4
DK_R = D_MODEL // H_R
DV_R = 2 * D_MODEL // H_R
D_V = H_R * DV_R
RET_IN_COLS = 2 * H_R * DK_R + 3 * D_V
RET_CHUNK = 128
ROPE_BASE = 10000.0


def rms_norm(x, g):
    xf = x.astype(jnp.float32)
    y = xf * lax.rsqrt(jnp.mean(xf * xf, axis=-1, keepdims=True) + NORM_EPS)
    return (y * g.astype(jnp.float32)).astype(x.dtype)

def swiglu_2(h, w_gate, w_up, w_down):
    return (jax.nn.silu(h @ w_gate) * (h @ w_up)) @ w_down

def t5_buckets(rel):
    half = NUM_BUCKETS // 2
    max_exact = half // 2
    n = np.abs(rel)
    large = max_exact + (np.log(np.maximum(n, 1) / max_exact)
                         / np.log(REL_MAX_DISTANCE / max_exact) * (half - max_exact)).astype(np.int64)
    large = np.minimum(large, half - 1)
    return ((rel > 0) * half + np.where(n < max_exact, n, large)).astype(np.int32)

def banded_attention(q, k, v, bias, radius):
    N, L, H, dh = q.shape
    nb = -(-L // BLK)
    Lp = nb * BLK
    qb = jnp.pad(q, ((0, 0), (0, Lp - L), (0, 0), (0, 0))).reshape(N, nb, BLK, H, dh)

    def windows(t):
        tp = jnp.pad(t, ((0, 0), (BLK, Lp - L + BLK), (0, 0), (0, 0))).reshape(N, nb + 2, BLK, H, dh)
        return jnp.concatenate([tp[:, :-2], tp[:, 1:-1], tp[:, 2:]], axis=2)

    kw, vw = windows(k), windows(v)
    a = np.arange(BLK)[:, None]
    c = np.arange(3 * BLK)[None, :]
    off = c - BLK - a
    key_pos = np.arange(nb)[:, None, None] * BLK - BLK + c[None]
    valid = (np.abs(off) <= radius)[None] & (key_pos >= 0) & (key_pos < L)
    bias_blk = bias[:, np.clip(off + radius, 0, 2 * radius)].astype(jnp.float32)

    s = jnp.einsum('nbqhd,nbkhd->nbhqk', qb, kw).astype(jnp.float32) * (dh ** -0.5) + bias_blk
    s = jnp.where(valid[None, :, None], s, NEG_INF)
    smax = jnp.max(s, axis=-1, keepdims=True)
    p = jnp.exp(s - smax)
    denom = jnp.sum(p, axis=-1, keepdims=True)
    o = jnp.einsum('nbhqk,nbkhd->nbqhd', (p / denom).astype(v.dtype), vw)
    lse = (smax + jnp.log(denom))[..., 0]
    o = o.reshape(N, Lp, H, dh)[:, :L]
    lse = lse.transpose(0, 1, 3, 2).reshape(N, Lp, H)[:, :L]
    return o, lse

def dilated_group(q, k, v, bias, dilation, radius):
    B, S, H, dh = q.shape
    Ls = S // dilation

    def split(t):
        return t.reshape(B, Ls, dilation, H, dh).transpose(0, 2, 1, 3, 4).reshape(B * dilation, Ls, H, dh)

    o, lse = banded_attention(split(q), split(k), split(v), bias, radius)
    o = o.reshape(B, dilation, Ls, H, dh).transpose(0, 2, 1, 3, 4).reshape(B, S, H, dh)
    lse = lse.reshape(B, dilation, Ls, H).transpose(0, 2, 1, 3).reshape(B, S, H)
    return o, lse

def dilated_attention(h, w_in, w_out, rel_bias):
    B, S, _ = h.shape
    proj = (h @ w_in).reshape(B, S, N_GROUPS, 3, H_A, DH_A)
    outs, lses = [], []
    for g, (window, dilation) in enumerate(DILATED_GROUPS):
        radius = window // (2 * dilation)
        buckets = t5_buckets(np.arange(-radius, radius + 1) * dilation)
        bias_g = rel_bias[g * H_A:(g + 1) * H_A][:, buckets]
        o, lse = dilated_group(proj[:, :, g, 0], proj[:, :, g, 1], proj[:, :, g, 2],
                               bias_g, dilation, radius)
        outs.append(o)
        lses.append(lse)
    wts = jax.nn.softmax(jnp.stack(lses, axis=0), axis=0)
    o = jnp.einsum('gbsh,gbshd->bshd', wts.astype(h.dtype), jnp.stack(outs, axis=0))
    return o.reshape(B, S, D_A) @ w_out

def rotary(t, pos):
    half = t.shape[-1] // 2
    inv_freq = 1.0 / (ROPE_BASE ** jnp.linspace(0.0, 1.0, half, dtype=jnp.float32))
    ang = pos[:, None] * inv_freq[None, :]
    cos = jnp.cos(ang)[None, :, None, :]
    sin = jnp.sin(ang)[None, :, None, :]
    t1, t2 = t[..., :half], t[..., half:]
    return jnp.concatenate([t1 * cos - t2 * sin, t1 * sin + t2 * cos], axis=-1)

def chunk_retention(q, k, v, log_gamma):
    B, S, H, dk = q.shape
    dv = v.shape[-1]
    C = RET_CHUNK
    n = S // C

    def to_chunks(t):
        return t.reshape(B, n, C, H, t.shape[-1]).transpose(1, 0, 3, 2, 4)

    qc, kc, vc = to_chunks(q), to_chunks(k), to_chunks(v)
    i = jnp.arange(C, dtype=jnp.float32)
    rel = i[:, None] - i[None, :]
    dmat = jnp.where(rel >= 0, jnp.exp(log_gamma[:, None, None] * jnp.maximum(rel, 0.0)), 0.0)
    inner = jnp.einsum('nbhid,nbhjd->nbhij', qc, kc) * dmat
    inner = jnp.einsum('nbhij,nbhje->nbhie', inner, vc)
    q_decay = jnp.exp(log_gamma[:, None] * (i + 1.0))[None, :, :, None]
    k_decay = jnp.exp(log_gamma[:, None] * (C - 1.0 - i))[None, :, :, None]
    chunk_decay = jnp.exp(log_gamma * C)[None, :, None, None]

    def step(state, xs):
        qi, ki, vi = xs
        cross = jnp.einsum('bhid,bhde->bhie', qi, state) * q_decay
        state = state * chunk_decay + jnp.einsum('bhjd,bhje->bhde', ki * k_decay, vi)
        return state, cross

    _, cross = lax.scan(step, jnp.zeros((B, H, dk, dv), jnp.float32), (qc, kc, vc))
    y = inner + cross
    return y.transpose(1, 0, 3, 2, 4).reshape(B, S, H, dv)

def head_group_norm(y):
    mu = jnp.mean(y, axis=-1, keepdims=True)
    var = jnp.mean(jnp.square(y - mu), axis=-1, keepdims=True)
    return (y - mu) * lax.rsqrt(var + NORM_EPS)

def retention(h, w_in, w_out, decay_logit):
    B, S, _ = h.shape
    proj = (h @ w_in).astype(jnp.float32)
    dq = H_R * DK_R
    q = proj[..., :dq].reshape(B, S, H_R, DK_R)
    k = proj[..., dq:2 * dq].reshape(B, S, H_R, DK_R)
    v = proj[..., 2 * dq:2 * dq + D_V].reshape(B, S, H_R, DV_R)
    g_f = proj[..., 2 * dq + D_V:2 * dq + 2 * D_V].reshape(B, S, H_R, DV_R)
    g_b = proj[..., 2 * dq + 2 * D_V:].reshape(B, S, H_R, DV_R)
    pos = jnp.arange(S, dtype=jnp.float32)
    q = rotary(q, pos)
    k = rotary(k, pos) * (DK_R ** -0.5)
    log_gamma = jnp.log1p(-jnp.exp(decay_logit.astype(jnp.float32)))
    y_f = chunk_retention(q, k, v, log_gamma[0])
    y_b = jnp.flip(chunk_retention(jnp.flip(q, 1), jnp.flip(k, 1), jnp.flip(v, 1), log_gamma[1]), 1)
    y = jax.nn.silu(g_f) * head_group_norm(y_f) + jax.nn.silu(g_b) * head_group_norm(y_b)
    return y.reshape(B, S, D_V).astype(h.dtype) @ w_out

def second_inputs(seed: int = 0) -> dict:
    key = jax.random.key(seed)
    ks = jax.random.split(key, 12)
    f32 = jnp.float32
    x = jax.random.normal(ks[0], (BATCH, SEQ, D_MODEL), f32)
    norm_gains = 1.0 + 0.05 * jax.random.normal(ks[1], (DEPTH, N_NORMS, D_MODEL), f32)
    ffn_w_gate = jax.random.normal(ks[2], (DEPTH, 2, D_MODEL, D_FF), f32) * D_MODEL ** -0.5
    ffn_w_up = jax.random.normal(ks[3], (DEPTH, 2, D_MODEL, D_FF), f32) * D_MODEL ** -0.5
    ffn_w_down = jax.random.normal(ks[4], (DEPTH, 2, D_FF, D_MODEL), f32) * D_FF ** -0.5
    attn_w_in = jax.random.normal(ks[5], (N_ATTN_LAYERS, D_MODEL, ATTN_IN_COLS), f32) * D_MODEL ** -0.5
    attn_w_out = jax.random.normal(ks[6], (N_ATTN_LAYERS, D_A, D_MODEL), f32) * D_A ** -0.5
    rel_bias = 0.5 * jax.random.normal(ks[7], (N_GROUPS * H_A, NUM_BUCKETS), f32)
    ret_w_in = jax.random.normal(ks[8], (N_RET_LAYERS, D_MODEL, RET_IN_COLS), f32) * D_MODEL ** -0.5
    ret_w_out = jax.random.normal(ks[9], (N_RET_LAYERS, D_V, D_MODEL), f32) * D_V ** -0.5
    base = -(5.0 + jnp.arange(H_R, dtype=f32)) * math.log(2.0)
    ret_decay_logit = base[None, None, :] + 0.1 * jax.random.normal(ks[10], (N_RET_LAYERS, 2, H_R), f32)
    return {"x": x, "norm_gains": norm_gains, "ffn_w_gate": ffn_w_gate, "ffn_w_up": ffn_w_up,
            "ffn_w_down": ffn_w_down, "attn_w_in": attn_w_in, "attn_w_out": attn_w_out,
            "rel_bias": rel_bias, "ret_w_in": ret_w_in, "ret_w_out": ret_w_out,
            "ret_decay_logit": ret_decay_logit}

def second_block(x, norm_gains, ffn_w_gate, ffn_w_up, ffn_w_down, attn_w_in, attn_w_out,
              rel_bias, ret_w_in, ret_w_out, ret_decay_logit):
    for i in range(DEPTH):
        g = norm_gains[i]
        h = swiglu_2(rms_norm(x, g[0]), ffn_w_gate[i, 0], ffn_w_up[i, 0], ffn_w_down[i, 0])
        x = x + 0.5 * rms_norm(h, g[1])
        hm = rms_norm(x, g[2])
        if i % N_MIXERS == 0:
            j = i // N_MIXERS
            m = dilated_attention(hm, attn_w_in[j], attn_w_out[j], rel_bias)
        else:
            j = i // N_MIXERS
            m = retention(hm, ret_w_in[j], ret_w_out[j], ret_decay_logit[j])
        x = x + rms_norm(m, g[3])
        h = swiglu_2(rms_norm(x, g[4]), ffn_w_gate[i, 1], ffn_w_up[i, 1], ffn_w_down[i, 1])
        x = x + 0.5 * rms_norm(h, g[5])
    return x


def setup_inputs(seed=0):
    out = dict(first_inputs(seed))
    for name, value in second_inputs(seed + 1).items():
        if name != "x":
            out[name + "_2"] = value
    return out


def reference(
    x, norm_g, w_in, mla_q_norm, mla_kv_norm, mla_w_uq, mla_w_ukv, swa_sinks, nsa_cmp_pos,
    nsa_cmp_w1, nsa_cmp_w2, diff_lambda, diff_subln, rel_bias_table, w_branch, w_gate, w_o,
    ffn_w_gate, ffn_w_up, ffn_w_down, final_g, norm_gains_2, ffn_w_gate_2, ffn_w_up_2,
    ffn_w_down_2, attn_w_in_2, attn_w_out_2, rel_bias_2, ret_w_in_2, ret_w_out_2,
    ret_decay_logit_2,
):
    x = first_block(
        x, norm_g, w_in, mla_q_norm, mla_kv_norm, mla_w_uq, mla_w_ukv, swa_sinks, nsa_cmp_pos,
        nsa_cmp_w1, nsa_cmp_w2, diff_lambda, diff_subln, rel_bias_table, w_branch, w_gate, w_o,
        ffn_w_gate, ffn_w_up, ffn_w_down, final_g,
    )
    return second_block(
        x, norm_gains_2, ffn_w_gate_2, ffn_w_up_2, ffn_w_down_2, attn_w_in_2, attn_w_out_2,
        rel_bias_2, ret_w_in_2, ret_w_out_2, ret_decay_logit_2,
    )


_drawn_inputs = setup_inputs


def setup_inputs(seed=0):
    import zlib

    import numpy as np

    out = dict(_drawn_inputs(seed))
    spreads = {}
    factors = {'mla_q_norm': 5.474, 'swa_sinks': 3.882}
    for name, (base, spread) in spreads.items():
        noise = np.random.default_rng([zlib.crc32(name.encode()), seed]).standard_normal(out[name].shape)
        drawn = base * np.exp(spread * noise) if base else spread * noise
        out[name] = jnp.asarray(drawn.astype(out[name].dtype))
    for name, factor in factors.items():
        out[name] = (out[name] * factor).astype(out[name].dtype)
    return out
```

```python
from contextlib import ExitStack
import math

import numpy as np

import concourse.bass as bass
from concourse import mybir

F32 = mybir.dt.float32
BF16 = mybir.dt.bfloat16
F32R = mybir.dt.float32r
ALU = mybir.AluOpType
ACT = mybir.ActivationFunctionType
AX_X = mybir.AxisListType.X

P = 128
SEQ = 256
TT = SEQ // P
D = 1024
KD = D // P
DEPTH = 2
D_FF = 2816
FT = D_FF // P
EPS = 1e-6
NEG = -1e30

SLOT = 3072
NS = 4
A_COLS = 384
T_PER_SLOT = SLOT // D

MLA_H, NOPE, ROPE, MLA_V = 8, 64, 32, 64
QK_M = NOPE + ROPE
HD = 64
CMP_LEN, CMP_STRIDE, CMP_HID = 32, 16, 128
NC = (SEQ - CMP_LEN) // CMP_STRIDE + 1
SWA_WINDOW = 128
N_BUCKETS, MAX_DIST = 32, 128

_SECT = dict(zip(
    "cq ckv krope sq sk sv nq nkc nvc nks nvs nkw nvw gate dq dk dv".split(),
    np.cumsum([0, 256, 128, 32, 512, 128, 128, 512, 128, 128, 128, 128, 128, 128, 24, 512, 512])))
ROW = dict(cq=0, ckv=256, sv=384, nvs=512, nvw=640, dv=768, krope=1280, gate=1312)
ROW_W = 1336
T_SQ, T_SK, T_NQ, T_CMP, T_KS, T_KW, T_DQ, T_DK, N_T = 0, 4, 5, 9, 11, 12, 13, 17, 21

NB2 = 32
N_GROUPS = 3
NV_2 = 12 * P
H_A = 16
RH, DK_R, DV_R = 4, 256, 512
D_V = RH * DV_R
QR_T = 16

C_FFN = FT
C_T = N_T // T_PER_SLOT
C_A = 4
C_MIX = 1 + 2 + C_T + C_A
C_GB = 16
C_WO = 3
C_LAYER = 2 * C_FFN + C_MIX + C_GB + C_WO
C_DIL = 3 * 8 + C_WO
C_RET_QK, C_RET_V, C_RET_O = 6, 16, 6
C_RET = C_RET_QK + C_RET_V + C_RET_O
N_SLOTS = DEPTH * C_LAYER + 4 * C_FFN + C_DIL + C_RET

RAW, WHOLE, MERGE, FFN = range(4)
_FFN = [FFN] * C_FFN
SLOT_KIND = (DEPTH * (_FFN + [WHOLE] * (C_A + C_T) + [RAW] * 3 + [MERGE] * C_GB + [RAW] * C_WO + _FFN)
             + _FFN + [WHOLE] * (3 * 8) + [RAW] * C_WO + _FFN
             + _FFN + [WHOLE] * (C_RET_QK + C_RET_V) + [RAW] * C_RET_O + _FFN)
assert len(SLOT_KIND) == N_SLOTS
SPLIT_SLOTS = [c for c in range(N_SLOTS) if SLOT_KIND[c] != RAW]
SPLIT_INDEX = {c: k for k, c in enumerate(SPLIT_SLOTS)}



def _bucket_5(dist):
    n = np.maximum(dist, 0)
    half = N_BUCKETS // 2
    nf = np.maximum(n, 1).astype(np.float32)
    large = half + (np.log(nf / np.float32(half)) / np.float32(math.log(MAX_DIST / half)) * np.float32(half)).astype(np.int32)
    return np.where(n < half, n, np.minimum(large, N_BUCKETS - 1))


def _bucket_2(rel):
    half, exact = NB2 // 2, NB2 // 4
    n = np.abs(rel)
    large = exact + (np.log(np.maximum(n, 1) / exact) / np.log(1024 / exact) * (half - exact)).astype(np.int64)
    large = np.minimum(large, half - 1)
    return ((rel > 0) * half + np.where(n < exact, n, large)).astype(np.int32)


def _onehot(bucket, valid):
    n = bucket.shape[0]
    out = np.zeros((33, n), np.float32)
    out[np.where(valid, bucket, 32), np.arange(n)] = 1.0
    return out


def constants():
    c = {}
    dist = 255 - np.arange(512)
    c["pick_window"] = _onehot(_bucket_5(dist), (dist >= 0) & (dist < SWA_WINDOW))
    c["pick_causal"] = _onehot(_bucket_5(dist), dist >= 0)
    m = np.arange(P) - 64
    inside = m > -64
    masked = _onehot(_bucket_2(m), m > 64)
    picks = [_onehot(_bucket_2(4 * m + d), (np.abs(4 * m + d) <= 64) & inside) for d in range(-3, 4)]
    for ok in (inside, inside & (m % 4 == 0)):
        picks += [masked, _onehot(_bucket_2(4 * m), ok)]
    picks.append(masked)
    c["pick_2"] = np.concatenate(picks, 1)
    i, j = np.arange(SEQ), np.arange(SEQ)
    rel = (i[None, :] - j[:, None]).astype(np.float32)
    parts = [np.maximum(rel, 0), np.maximum(-rel, 0), rel >= 0, rel <= 0]
    parts = [t.astype(np.float32).reshape(TT, P, SEQ).transpose(1, 0, 2).reshape(P, TT * SEQ) for t in parts]
    inv = 1.0 / (np.float32(10000.0) ** np.linspace(0.0, 1.0, P, dtype=np.float32))
    ang = inv.astype(np.float32)[:, None] * np.arange(SEQ, dtype=np.float32)[None]
    c["ret_const"] = np.concatenate(parts + [np.cos(ang), np.sin(ang)], 1).astype(np.float32)
    pos = np.arange(SEQ, dtype=np.float32)
    freqs = (np.float32(10000.0) ** (-np.arange(16, dtype=np.float32) / np.float32(16))).astype(np.float32)
    ang = pos[:, None] * freqs
    tab = np.stack([np.cos(ang), np.sin(ang)], 1).astype(np.float32)
    c["rope"] = tab.reshape(TT, P, 32).transpose(1, 0, 2).reshape(P, 64)
    q = np.arange(SEQ)
    ok = (np.arange(NC) * CMP_STRIDE + CMP_LEN - 1)[None] <= q[:, None]
    ok = ok.reshape(TT, P, NC).transpose(1, 0, 2).reshape(P, TT * NC)
    c["cmp_mask"] = np.concatenate([np.where(ok, 0.0, NEG), ok.astype(np.float32)], 1).astype(np.float32)
    c["ident"] = np.eye(P, dtype=np.float32)
    sel = np.zeros((P, 8 * NC + 8), np.float32)
    for h in range(8):
        for b in range(NC):
            sel[b, h * NC + b] = 1.0
            sel[h * NC + b, 8 * NC + h] = 1.0
    c["cmp_sel"] = sel
    return c


CONST_NAMES = ["ident", "rope", "cmp_mask", "cmp_sel"]
CONST_W = dict(ident=128, rope=64, cmp_mask=2 * TT * NC, cmp_sel=8 * NC + 8)


def build(nc, stream, x_rows, norm_gT_2, gains_2, table_2, pick_2, ret_const, decay, norm_gT, mla_gT, sinks, posT, lam, subln, table_1, consts, flip_dram, pick_1, out):
    ctx = ExitStack()
    with ctx:
        def sb(name, shape, dt=F32):
            return ctx.enter_context(nc.sbuf_tensor(name, shape, dt))

        def sem(name):
            return ctx.enter_context(nc.semaphore(name))

        ring = sb("ring", [P, NS, SLOT])
        ring_offset = nc.sbuf_base - NS * SLOT * 4
        ring_lo = nc.alloc_sbuf_tensor_at("ring_lo", [P, NS, SLOT], F32R, offset=ring_offset, align_bytes=32)
        ring_hi = sb("ring_hi", [P, 2, SLOT], F32R)
        h = sb("h", [P, TT, D])
        xn = sb("xn", [P, TT, D])
        uTh = sb("uTh", [P, KD, SEQ], F32R)
        uTl = sb("uTl", [P, KD, SEQ], F32R)
        hid_hi = sb("hid_hi", [P, 2, SEQ], F32R)
        hid_lo = sb("hid_lo", [P, 2, SEQ], F32R)
        bias = sb("bias", [P, 21, SEQ])
        qkT = sb("qkT", [P, N_T, SEQ])
        row = sb("row", [P, TT, ROW_W])
        yR = sb("yR", [P, 4, TT, 512])
        work_all = sb("work_all", [P, 2560])
        work = work_all[:, 0:6 * 384].rearrange("p (n c) -> p n c", n=6)
        mlaT_all = sb("mlaT_all", [P, MLA_H, 512])
        cst = sb("cst", [P, sum(CONST_W.values())])
        norm_g = sb("norm_g", [P, DEPTH, 3, KD])
        mla_g = sb("mla_g", [P, DEPTH, 3])
        sink = sb("sink", [P, DEPTH, 8])
        pos = sb("pos", [P, DEPTH, CMP_LEN])
        sub = sb("sub", [P, DEPTH, P])
        zero_bf = sb("zero_bf", [1, P], BF16)
        ssq = sb("ssq", [P, 8])
        rsq = sb("rsq", [P, 8])
        half_neg = sb("half_neg", [P, 8])
        small = sb("small", [P, 4, 14])
        norm_g2 = sb("norm_g2", [P, DEPTH, 3, KD])
        lg = sb("lg", [P, 5, 8])
        stats = sb("stats", [P, 4, 6])
        moments = sb("moments", [P, 4, 2])
        nlam = sb("nlam", [P, DEPTH, 4])
        gates = sb("gates", [P, TT, 24])
        cmps = sb("cmps", [P, 2 * NC])

        at = {}
        o = 0
        for name in CONST_NAMES:
            at[name] = cst[:, o:o + CONST_W[name]]
            o += CONST_W[name]
        ident = at["ident"]
        rope = at["rope"].rearrange("p (t c i) -> p t c i", t=TT, c=2)
        cmp_neg = at["cmp_mask"][:, 0:TT * NC].rearrange("p (t c) -> p t c", t=TT)
        cmp_ok = at["cmp_mask"][:, TT * NC:].rearrange("p (t c) -> p t c", t=TT)
        cmp_sel = at["cmp_sel"][0:NC, 0:8 * NC]
        head_of_row = at["cmp_sel"][0:8 * NC, 8 * NC:8 * NC + 8]
        mlaT = mlaT_all[0:QK_M, :, :]
        prod = work_all[:, 0:512].rearrange("p (n c) -> p n c", n=2)
        sil = work_all[:, 512:1024].rearrange("p (n c) -> p n c", n=2)
        yT = qkT[:, 0:16, :].rearrange("p (b f) t -> p b f t", b=4)
        mT = row[:, :, :].rearrange("p a b -> p (a b)")[:, 0:KD * SEQ].rearrange("p (k t) -> p k t", k=KD)
        flatY = yR[:, :, :, :].rearrange("p a b c -> p (a b c)")
        qR = flatY[:, 0:TT * 768].rearrange("p (t n) -> p t n", t=TT)
        kR = flatY[:, TT * 768:2 * TT * 768].rearrange("p (t n) -> p t n", t=TT)
        flatW = work_all
        cT = flatW[:, 0:768].rearrange("p (f t) -> p f t", f=3)
        ropet = flatW[:, 768:768 + 512].rearrange("p (n h i) -> p n h i", n=4, h=8)
        kr = flatW[:, 1280:1344].rearrange("p (t i) -> p t i", t=TT)
        blk = flatW[:, 0:CMP_LEN * 2 * NC].rearrange("p (l h c) -> p l h c", l=CMP_LEN, h=2)
        hidC = flatW[:, 960:1020].rearrange("p (w n) -> p w n", w=2)
        vc = flatW[:, 1024:1152]
        vB = flatW[:, 1152:1664].rearrange("p (h d) -> p h d", h=8)
        cs = flatW[:, 1664:1904].rearrange("p (t h c) -> p t h c", t=TT, h=8)
        ce = flatW[:, 1904:2144].rearrange("p (t h c) -> p t h c", t=TT, h=8)
        pcT = flatW[:, 2144:2400]
        cden = flatW[:, 2400:2448].rearrange("p (n m) -> p n m", n=3)
        xn_flat = xn[:, :, :].rearrange("p a b -> p (a b)")
        lamb = xn_flat[:, 1024:1536].rearrange("p (l n d) -> p l n d", l=DEPTH, n=4)
        mlaV = xn_flat[:, 1024:2048].rearrange("p (t n) -> p t n", t=TT)
        gains = bias[:, 0:20, :].rearrange("p a b -> p (a b)").rearrange("p (n d) -> p n d", n=5)
        gain_rows = [gains[:, n, :] for n in range(5)] + [flatY[:, 2048:3072], flatY[:, 3072:4096]]
        flatM = mlaT_all[:, :, :].rearrange("p a b -> p (a b)")
        flatR = row[:, :, :].rearrange("p a b -> p (a b)")
        flatB = bias[:, :, :].rearrange("p a b -> p (a b)")
        picks_2 = flatM[0:33, 0:NV_2]
        table_2_sb = flatM[0:33, NV_2:NV_2 + 48]
        vec_2_sb = work_all[0:16, 0:NV_2]
        hankel_2 = flatM[:, 0:2560].rearrange("p (n c) -> p n c", n=4)
        flip_2 = flatM[:, 2560:2688]
        qkD = qkT[:, 0:12, :].rearrange("p (b n) t -> p b n t", b=2)
        vD = flatR[:, 0:1536].rearrange("p (b t n) -> p b t n", b=2, t=TT)
        yD = flatY[:, 0:2048].rearrange("p (t n) -> p t n", t=TT)
        probs = work_all[:, 0:1024].rearrange("p (b c) -> p b c", b=2)
        probsT = work_all[:, 1024:2048].rearrange("p (b c) -> p b c", b=2)
        rel = flatR[:, 0:1024].rearrange("p (d c) -> p d c", d=2)
        rel_ok = flatR[:, 1024:2048].rearrange("p (d c) -> p d c", d=2)
        rcos, rsin = flatR[:, 2048:2304], flatR[:, 2304:2560]
        decays = flatY[:, 0:1024].rearrange("p (d c) -> p d c", d=2)
        yH = flatY[:, 1024:2048].rearrange("p (t n) -> p t n", t=TT)
        swish = [flatB[:, n * 2048:(n + 1) * 2048].rearrange("p (t n) -> p t n", t=TT) for n in range(2)]
        vH = [flatB[:, 4096:5120].rearrange("p (t n) -> p t n", t=TT),
              xn_flat[:, 0:1024].rearrange("p (t n) -> p t n", t=TT)]
        inner = work_all[:, 0:1024].rearrange("p (d t i) -> p d t i", d=2, t=TT)
        tmpH = work_all[:, 1024:2560].rearrange("p (n c) -> p n c", n=3)
        yT_2 = flatM[:, :].rearrange("p (k t) -> p k t", k=16)
        hankel = [flatY, row[:, :, :].rearrange("p a b -> p (a b)")]
        flip = xn_flat[:, 1600:1600 + P]
        picks_sb = qkT[:, 0:4, :].rearrange("p a b -> p (a b)")
        table_sb = qkT[0:33, 4, 0:21]
        vec_sb = qkT[:, 5:9, :].rearrange("p a b -> p (a b)")

        ps = ctx.enter_context(nc.psum_tensor("ps", [P, 8, 512], F32))
        vecs_2 = nc.dram_tensor("bias_vectors_2", (16, NV_2), F32, kind="Internal").ap()
        vecs = nc.dram_tensor("bias_vectors", (21, 512), F32, kind="Internal").ap()

        weights_in = [sem(f"weights_in_{s}") for s in range(NS)]
        ring_used = sem("ring_used")
        params_in = sem("params_in")
        picks_in = sem("picks_in")
        table_masked = sem("table_masked")
        vec_ready = sem("vec_ready")
        vec_copied = sem("vec_copied")
        vec_stored = sem("vec_stored")
        hankel_in = sem("hankel_in")
        bias_psum = sem("bias_psum")
        bias_ready = sem("bias_ready")
        filled = sem("filled")
        stage_done = sem("stage_done")
        dve_chain = sem("dve_chain")
        act_chain = sem("act_chain")
        squares_ready = sem("squares_ready")
        mean_ready = sem("mean_ready")
        inv_root_ready = sem("inv_root_ready")
        xn_dve_ready = sem("xn_dve_ready")
        xn_act_ready = sem("xn_act_ready")
        xT_ready = sem("xT_ready")
        uT_dve_ready = sem("uT_dve_ready")
        uT_act_ready = sem("uT_act_ready")
        gu_ready = sem("gu_ready")
        silu_ready = sem("silu_ready")
        prod_ready = sem("prod_ready")
        hid_hi_ready = sem("hid_hi_ready")
        hi_ready = sem("hi_ready")
        lo_ready = sem("lo_ready")
        hidden_ready = sem("hidden_ready")
        piece_ready = sem("piece_ready")
        piece_act_out = sem("piece_act_out")
        piece_dve_out = sem("piece_dve_out")
        mla_squares = sem("mla_squares")
        mla_mean = sem("mla_mean")
        mla_inv = sem("mla_inv")
        mla_normed = sem("mla_normed")
        mla_cT_psum = sem("mla_cT_psum")
        mla_cT = sem("mla_cT")
        mla_roped = sem("mla_roped")
        gains_in = sem("gains_in")
        params_2_in = sem("params_2_in")
        table_2_masked = sem("table_2_masked")
        vec_2_ready = sem("vec_2_ready")
        vec_2_copied = sem("vec_2_copied")
        vec_2_stored = sem("vec_2_stored")
        flip_2_in = sem("flip_2_in")
        hankel_2_in = [sem(f"hankel_2_in_{n}") for n in range(4)]
        head_scored = sem("head_scored")
        max_2_ready = sem("max_2_ready")
        scores_2 = sem("scores_2")
        exp_2_done = sem("exp_2_done")
        turned_2 = sem("turned_2")
        pT_2_ready = sem("pT_2_ready")
        out_2 = sem("out_2")
        stored_2 = sem("stored_2")
        ret_const_in = sem("ret_const_in")
        decay_exp = sem("decay_exp")
        decay_one_minus = sem("decay_one_minus")
        decay_ln = sem("decay_ln")
        decay_ready = sem("decay_ready")
        ret_rotated = sem("ret_rotated")
        ret_scores = sem("ret_scores")
        ret_exp = sem("ret_exp")
        ret_inner = sem("ret_inner")
        ret_y = sem("ret_y")
        ret_moments = sem("ret_moments")
        ret_inv = sem("ret_inv")
        ret_swish = sem("ret_swish")
        ret_head = sem("ret_head")
        gates_ready = sem("gates_ready")
        blocks_ready = sem("blocks_ready")
        cmp_hidden = sem("cmp_hidden")
        cmp_gelu = sem("cmp_gelu")
        cmp_kv = sem("cmp_kv")
        cmp_kv_out = sem("cmp_kv_out")
        cmp_spread = sem("cmp_spread")
        cmp_vB = sem("cmp_vB")
        cmp_scores = sem("cmp_scores")
        cmp_shifted = sem("cmp_shifted")
        cmp_exp = sem("cmp_exp")
        cmp_probs = sem("cmp_probs")
        cmp_pT_psum = sem("cmp_pT_psum")
        cmp_pT = sem("cmp_pT")
        cmp_out = sem("cmp_out")
        lam_sums = sem("lam_sums")
        lam_exps = sem("lam_exps")
        scores_ready = sem("scores_ready")
        biased = sem("biased")
        negmax_ready = sem("negmax_ready")
        exp_done = sem("exp_done")
        probs_turned = sem("probs_turned")
        pT_ready = sem("pT_ready")
        attn_out = sem("attn_out")
        attn_stored = sem("attn_stored")
        diff_sq = sem("diff_sq")
        diff_inv = sem("diff_inv")
        gb_ready = sem("gb_ready")
        sig_ready = sem("sig_ready")
        merged = sem("merged")
        wo_ready = sem("wo_ready")
        x_stored = sem("x_stored")

        block = ctx.enter_context(nc.Block())
        STAGE_ENGINES = 4
        PARAM_DMAS = 9

        def layer_slot(l):
            return l * C_LAYER

        def merge_slot(l):
            return layer_slot(l) + C_FFN + C_MIX

        C2 = DEPTH * C_LAYER
        MIX_2 = [C_DIL, C_RET]
        HEADS_2 = 16
        NU2 = HEADS_2 * TT

        def layer_slot_2(i):
            return C2 + i * (2 * C_FFN + C_DIL)

        PIECES_DIL = 2 * (N_T + TT * C_A + 8 + MLA_H + 8)
        PIECES_RET = PIECES_DIL + 8 * 8 + 4
        RET_PIECES = ([("qk", t) for t in range(16)] + [("row", 0, n) for n in range(8)]
                      + [("row", 1, n) for n in range(8)]
                      + [("row", 2, n) for n in range(8)] + [("turn", 0, n) for n in range(2)]
                      + [("row", 3, n) for n in range(8)] + [("turn", 1, n) for n in range(2)]
                      + [("turn", 2, n) for n in range(2)] + [("turn", 3, n) for n in range(2)])

        def dilated_copy(g):
            n, bank = (g - PIECES_DIL) % 8, ps[:, 6 + g % 2, :]
            b = ((g - PIECES_DIL) // 8) % 2
            if n < 6:
                return qkD[:, b, n, :], bank[:, 0:SEQ], (HD ** -0.5 if n % 2 == 0 else None)
            return vD[:, b, n - 6, :], bank[:, 0:A_COLS], None

        def dilated_turn_copy(g):
            kp, bank = g - (PIECES_DIL + 64), ps[:, 6 + g % 2, :]
            return (mT[:, 2 * kp:2 * kp + 2, :].rearrange("p k (j r) -> p k r j", r=4),
                    bank.rearrange("p (k r j) -> p k r j", k=2, r=4), None)

        def retention_copy(g):
            what, bank = RET_PIECES[g - PIECES_RET], ps[:, 6 + g % 2, :]
            if what[0] == "qk":
                return qkT[:, what[1], :], bank[:, 0:SEQ], None
            hh, n = what[1:]
            if what[0] == "turn":
                k = 4 * hh + 2 * n
                return yT_2[:, k:k + 2, :].rearrange("p k t -> p (k t)"), bank, None
            a, tt = n // 2, n % 2
            return (None, (hh, a, tt), bank)

        def retention_row_parts(hh, a, tt, bank):
            out, o = [], a * A_COLS
            while o < (a + 1) * A_COLS:
                end = min((a + 1) * A_COLS, 1024 if o < 1024 else 1536)
                src = bank[:, o - a * A_COLS:end - a * A_COLS]
                out.append((swish[hh % 2][:, tt, o:end] if o < 1024 else vH[hh % 2][:, tt, o - 1024:end - 1024], src))
                o = end
            return out

        def units():
            out = []
            for n in range(8):
                out.append(dict(kind="mla", k=QK_M, scale=QK_M ** -0.5, bias=20, head=n))
            for n in range(8):
                out.append(dict(kind="swa", k=HD, scale=HD ** -0.5, bias=n, head=n))
            for kind in ("sel", "win"):
                for n in range(8):
                    out.append(dict(kind=kind, k=HD, scale=HD ** -0.5, bias=8 + n, head=n))
            for n in range(8):
                out.append(dict(kind="diff", k=HD, scale=HD ** -0.5, bias=16 + n // 2, head=n // 2, map=n % 2))
            return out

        UNITS = units()
        NU = len(UNITS)

        def unit_q(u):
            kind, n = u["kind"], u["head"]
            if kind == "mla":
                return mlaT[:, n, 0:SEQ]
            if kind == "diff":
                return qkT[64 * u["map"]:64 * u["map"] + 64, T_DQ + n, :]
            base = T_SQ if kind == "swa" else T_NQ
            return qkT[64 * (n // 4):64 * (n // 4) + 64, base + n % 4, :]

        def unit_k(u):
            kind, n = u["kind"], u["head"]
            if kind == "mla":
                return mlaT[:, n, SEQ:2 * SEQ]
            if kind == "diff":
                return qkT[64 * u["map"]:64 * u["map"] + 64, T_DK + n, :]
            tile = {"swa": T_SK, "sel": T_KS, "win": T_KW}[kind]
            return qkT[64 * (n // 4):64 * (n // 4) + 64, tile, :]

        def unit_v(u, kt):
            kind, n = u["kind"], u["head"]
            if kind == "mla":
                return mlaV[:, kt, 64 * n:64 * n + 64]
            if kind == "diff":
                return row[:, kt, ROW["dv"] + P * n:ROW["dv"] + P * n + P]
            o = ROW[{"swa": "sv", "sel": "nvs", "win": "nvw"}[kind]] + 64 * (n // 4)
            return row[:, kt, o:o + 64]

        def unit_y(u, qt):
            branch = {"mla": 0, "swa": 1, "sel": 2, "win": 2, "diff": 3}[u["kind"]]
            w = P if u["kind"] == "diff" else 64
            return yR[:, branch, qt, w * u["head"]:w * u["head"] + w]

        N_PIECES_PROJ = N_T + TT * C_A
        N_PIECES_MLA = 8 + MLA_H
        PIECES_LAYER = N_PIECES_PROJ + N_PIECES_MLA + 8

        def piece_copied(n):
            return (piece_act_out if n % 2 == 0 else piece_dve_out), n // 2 + 1

        VEC_2_PARTS = [(0, 512, 0), (512, 384, 0), (896, 384, 1), (1280, 256, 2)]

        def turned_places(u, k, src, residues):
            if not residues:
                return u[:, k, :], src
            return u[:, k, :].rearrange("p (r j) -> p j r", r=4), src.rearrange("p (j r) -> p j r", r=4)

        def high(c):
            return ring_hi[:, SPLIT_INDEX[c] % 2, :]

        def split_part(c, x):
            kind = SLOT_KIND[c]
            if kind == MERGE:
                return x.rearrange("p (n w) -> p n w", n=2)[:, :, 0:D]
            return x[:, 0:2 * D] if kind == FFN else x

        def split_after(c, ahead, end):
            if c + 2 < end:
                ahead(c + 2)

        def bias_parts():
            flat = bias[:, :, :].rearrange("p h k -> p (h k)")
            return [(flat[:, o:min(o + 512, 21 * SEQ)], min(512, 21 * SEQ - o)) for o in range(0, 21 * SEQ, 512)]

        def proj_copies(n, g):
            if n < TT * C_A:
                a, tt = n // 2, n % 2
                w = min(A_COLS, ROW_W - a * A_COLS)
                return row[:, tt, a * A_COLS:a * A_COLS + w], ps[:, g % 4, 0:w]
            return qkT[:, n - TT * C_A, :], ps[:, g % 4, 0:SEQ]

        def mla_copies(n, g):
            if n < 4:
                return qR[:, n // 2, (n % 2) * 384:(n % 2) * 384 + 384], ps[:, g % 4, 0:384]
            if n < 8:
                tt = (n - 4) // 2
                if n % 2:
                    return mlaV[:, tt, :], ps[:, g % 4, :]
                return (kR[:, tt, :].rearrange("p (h i) -> p h i", h=MLA_H)[:, :, 0:NOPE],
                        ps[:, g % 4, :].rearrange("p (h i) -> p h i", h=MLA_H))
            return mlaT[:, n - 8, :], ps[0:QK_M, g % 4, :]

        def done_projection(l, n, take):
            c0 = layer_slot(l) + C_FFN
            if n < TT * C_A:
                if n % TT == TT - 1:
                    split_after(c0 + n // TT, take, c0 + C_A + C_T)
            elif (n - TT * C_A) % T_PER_SLOT == T_PER_SLOT - 1:
                split_after(c0 + C_A + (n - TT * C_A) // T_PER_SLOT, take, c0 + C_A + C_T)

        def done_dilated(n, take):
            c0 = layer_slot_2(0) + C_FFN
            if n % 8 in (2, 5, 7):
                split_after(c0 + 3 * (n // 8) + (2, 5, 7).index(n % 8), take, c0 + 3 * 8)

        def done_retention(g, take):
            c0 = layer_slot_2(1) + C_FFN
            end = c0 + C_RET_QK + C_RET_V
            what = RET_PIECES[g - PIECES_RET]
            if what[0] == "qk":
                if what[1] % T_PER_SLOT == T_PER_SLOT - 1 or what[1] == QR_T - 1:
                    split_after(c0 + what[1] // T_PER_SLOT, take, end)
            elif what[0] == "row" and what[2] % TT == TT - 1:
                split_after(c0 + C_RET_QK + C_A * what[1] + what[2] // TT, take, end)

        def branch_copies(n, g):
            return (yT[:, n // 2, 2 * (n % 2):2 * (n % 2) + 2, :].rearrange("p f t -> p (f t)"), ps[:, g % 4, :])


        @block.sync
        def _(sp):
            def load(c_dram, s):
                return sp.dma_start(ring[:, s, :], c_dram).then_inc(weights_in[s], 16)

            sp.wait_ge(table_masked, 1)
            sp.dma_start(table_sb[0:32, 0:20], table_1).then_inc(picks_in, 16)
            for n in range(2):
                sp.dma_start(picks_sb[0:33, 512 * n:512 * n + 512], pick_1[:, 512 * n:512 * n + 512]).then_inc(picks_in, 16)
            for s in range(NS):
                load(stream[s, :, :], s)
            rounds = N_SLOTS // NS
            with sp.Fori(1, rounds) as r:
                for s in range(NS):
                    sp.wait_ge(ring_used, r * NS + (s + 1 - NS))
                    load(stream[bass.ds(r * NS + s, 1), :, :].rearrange("o p n -> (o p) n"), s)
            for c in range(rounds * NS, N_SLOTS):
                sp.wait_ge(ring_used, c + 1 - NS)
                load(stream[c, :, :], c % NS)

        def boundary(eng, n):
            eng.drain().then_inc(stage_done, 1)
            eng.wait_ge(stage_done, STAGE_ENGINES * (n + 1))

        @block.tensor
        def _(pe):
            pending = [0]
            stage = [0]

            def weights(c, i=None):
                v = 16 * (c // NS + 1)
                pe.wait_ge(weights_in[c % NS], v if i is None else 16 * i + v)

            def slot(c):
                return ring[:, c % NS, :]

            def low(c):
                return ring_lo[:, c % NS, :]

            def split_weights(c, i=None):
                v = SPLIT_INDEX[c] + 1
                pe.wait_ge(lo_ready, v if i is None else NS * i + v)

            def stationary_weights(out_, c, cols, k, start, stop):
                mm(out_, high(c)[:, cols], uTh[:, k, :], start, False)
                mm(out_, high(c)[:, cols], uTl[:, k, :], False, False)
                return mm(out_, low(c)[:, cols], uTh[:, k, :], False, stop)

            def moving_weights(out_, c, cols, k, tt, start, stop):
                ts = slice(tt * P, (tt + 1) * P)
                mm(out_, uTh[:, k, ts], high(c)[:, cols], start, False)
                mm(out_, uTh[:, k, ts], low(c)[:, cols], False, False)
                return mm(out_, uTl[:, k, ts], high(c)[:, cols], False, stop)

            def mm(out_, lhsT, rhs, start, stop, **kw):
                m = pe.matmul(out_, lhsT, rhs, start=start, stop=stop, **kw)
                if pending[0]:
                    m.then_inc(ring_used, pending[0])
                    pending[0] = 0
                return m

            def end_stage():
                if pending[0]:
                    pe.drain().then_inc(ring_used, pending[0])
                    pending[0] = 0
                boundary(pe, stage[0])
                stage[0] += 1

            def norm(n):
                pe.wait_ge(xn_dve_ready, n + 1)
                pe.wait_ge(xn_act_ready, n + 1)
                for kp in range(KD // 2):
                    for j in range(2):
                        for tt in range(TT):
                            k = 2 * kp + j
                            last = pe.transpose(ps[:, 4 + kp, j * SEQ + tt * P:j * SEQ + tt * P + P],
                                                xn[:, tt, k * P:(k + 1) * P], ident)
                    last.then_inc(xT_ready, 1)

            def ffn(f, c0, n):
                def gate_up(c, t, i=None, first=False):
                    split_weights(c, i)
                    for part in range(2):
                        for k in range(KD):
                            if first and part == 0:
                                pe.wait_ge(uT_dve_ready, KD * n + max(2, k + 1))
                            last = stationary_weights(ps[:, 4 + t % 2, part * SEQ:(part + 1) * SEQ], c,
                                                      slice(part * D + k * P, part * D + (k + 1) * P), k,
                                                      k == 0, k == KD - 1)
                    last.then_inc(gu_ready, 1)

                def down(c, t, i=None, stop=False):
                    v = FT * f + (c - c0) + 1
                    pe.wait_ge(hidden_ready, v if i is None else NS * i + v)
                    for tt in range(TT):
                        for half in range(2):
                            cols = slice(2 * D + half * 512, 2 * D + half * 512 + 512)
                            x_hi, x_lo = (x[:, t % 2, tt * P:(tt + 1) * P] for x in (hid_hi, hid_lo))
                            for x, w in ((x_hi, high(c)), (x_hi, low(c)), (x_lo, high(c))):
                                last = pe.matmul(ps[:, tt * 2 + half, :], x, w[:, cols], start=False,
                                                 stop=stop and x is x_lo, skip_group_check=True)
                    last.then_inc(ring_used, 1)

                for b in range(4):
                    pe.matmul(ps[:, b, :], zero_bf[:, :], zero_bf[:, 0:1].to_broadcast([1, 512]),
                              start=True, stop=False, skip_group_check=True)
                gate_up(c0, 0, first=True)
                with pe.Fori(0, FT // NS) as i:
                    for t in range(NS):
                        gate_up(c0 + t + 1, t + 1, i)
                        down(c0 + t, t, i)
                gate_up(c0 + FT - 1, FT - 1)
                down(c0 + FT - 2, FT - 2)
                down(c0 + FT - 1, FT - 1, None, True)

            def piece_bank(n):
                if n >= 4:
                    s, v = piece_copied(n - 4)
                    pe.wait_ge(s, v)
                return ps[:, n % 4, :]

            def projections(l, n):
                c0 = layer_slot(l) + C_FFN
                pc = l * PIECES_LAYER
                for a in range(C_A):
                    c = c0 + a
                    split_weights(c)
                    w = min(A_COLS, ROW_W - a * A_COLS)
                    for tt in range(TT):
                        bank = piece_bank(pc)
                        for k in range(KD):
                            if a == 0 and tt == 0:
                                pe.wait_ge(uT_dve_ready, KD * n + k + 1)
                            last = moving_weights(bank[:, 0:w], c, slice(k * A_COLS, k * A_COLS + w), k, tt,
                                                  k == 0, k == KD - 1)
                        last.then_inc(piece_ready, 1)
                        pc += 1
                    pending[0] += 1
                for t in range(N_T):
                    c = c0 + C_A + t // T_PER_SLOT
                    split_weights(c)
                    bank = piece_bank(pc)
                    o = (t % T_PER_SLOT) * D
                    for k in range(KD):
                        last = stationary_weights(bank[:, 0:SEQ], c, slice(o + k * P, o + (k + 1) * P), k,
                                                  k == 0, k == KD - 1)
                    last.then_inc(piece_ready, 1)
                    pc += 1
                    if t % T_PER_SLOT == T_PER_SLOT - 1:
                        pending[0] += 1

            def mla(l):
                c = layer_slot(l) + C_FFN + C_A + C_T
                pc = l * PIECES_LAYER + N_PIECES_PROJ
                pe.wait_ge(mla_normed, l + 1)
                for f in range(3):
                    for tt in range(TT):
                        last = pe.transpose(ps[:, 4 + f, tt * P:(tt + 1) * P], xn_flat[:, (tt * 3 + f) * P:(tt * 3 + f + 1) * P], ident)
                last.then_inc(mla_cT_psum, 1)
                pe.wait_ge(mla_cT, l + 1)
                weights(c)
                w_uq = slot(c)[:, 0:1536].rearrange("p (k n) -> p k n", k=2)
                w_ukv = slot(c)[:, 1536:2560]
                for tt in range(TT):
                    for half in range(2):
                        bank = piece_bank(pc)
                        for k in range(2):
                            last = mm(bank[:, 0:384], cT[:, k, tt * P:(tt + 1) * P],
                                      w_uq[:, k, half * 384:(half + 1) * 384], k == 0, k == 1)
                        last.then_inc(piece_ready, 1)
                        pc += 1
                for tt in range(TT):
                    for half in range(2):
                        bank = piece_bank(pc)
                        pe.matmul(bank, cT[:, 2, tt * P:(tt + 1) * P], w_ukv[:, half * 512:(half + 1) * 512],
                                  start=True, stop=True).then_inc(piece_ready, 1)
                        pc += 1
                pe.wait_ge(mla_roped, l + 1)
                for n in (pc - 1, pc - 2):
                    s, v = piece_copied(n)
                    pe.wait_ge(s, v)
                for n in range(MLA_H):
                    bank = piece_bank(pc)
                    for j, src in enumerate((qR, kR)):
                        for tt in range(TT):
                            last = pe.transpose(bank[0:QK_M, j * SEQ + tt * P:j * SEQ + tt * P + P],
                                                src[:, tt, n * QK_M:(n + 1) * QK_M], ident)
                    last.then_inc(piece_ready, 1)
                    pc += 1

            def compress(l):
                c2 = layer_slot(l) + C_FFN + C_A + C_T
                pe.wait_ge(blocks_ready, l + 1)
                for half in range(2):
                    c = c2 + 1 + half
                    weights(c)
                    for l_ in range(16):
                        pos_ = half * 16 + l_
                        for w in range(2):
                            r = slice(64 * w, 64 * w + 64)
                            last = pe.matmul(ps[:, 6 + w, 0:2 * NC], slot(c)[r, l_ * P:(l_ + 1) * P],
                                             blk[r, pos_, :, :], start=pos_ == 0, stop=pos_ == 31,
                                             skip_group_check=True)
                last.then_inc(cmp_hidden, 1)
                pe.wait_ge(cmp_gelu, l + 1)
                w2 = slot(c2)[:, 2560:2752]
                mm(ps[:, 4, 0:2 * NC], w2[:, 0:P], hidC[:, 0, :], True, True)
                for n in range(2):
                    last = mm(ps[0:NC, 5, n * 64:n * 64 + 64], hidC[:, 1, n * NC:(n + 1) * NC],
                              w2[:, P:P + 64], True, True)
                last.then_inc(cmp_kv, 1)
                pending[0] += 3
                pe.wait_ge(cmp_kv_out, l + 1)
                pe.matmul(ps[0:8 * NC, 6, 0:P], cmp_sel, vc[0:NC, :], start=True, stop=True).then_inc(cmp_spread, 1)
                for n in range(8):
                    r = slice(64 * (n // 4), 64 * (n // 4) + 64)
                    for tt in range(TT):
                        o = (tt * 4 + n % 4) * NC
                        last = mm(ps[:, 7 - 2 * (n // 4), o:o + NC], qkT[r, T_NQ + n % 4, tt * P:(tt + 1) * P],
                                  cmps[r, (n // 4) * NC:(n // 4) * NC + NC], True, True)
                last.then_inc(cmp_scores, 1)
                pe.wait_ge(cmp_probs, l + 1)
                for tt in range(TT):
                    last = pe.transpose(ps[0:8 * NC, 4, tt * P:(tt + 1) * P],
                                        ce[:, tt, :, :].rearrange("p h c -> p (h c)"), ident)
                last.then_inc(cmp_pT_psum, 1)
                pe.wait_ge(cmp_pT, l + 1)
                pe.wait_ge(cmp_vB, l + 1)
                for tt in range(TT):
                    last = mm(ps[:, 5 + tt, :], pcT[0:8 * NC, tt * P:(tt + 1) * P],
                              vB[0:8 * NC, :, :].rearrange("p h d -> p (h d)"), True, True)
                last.then_inc(cmp_out, 1)

            def scores(a, u):
                if a >= 2:
                    pe.wait_ge(biased, a - 1)
                q, k = unit_q(u), unit_k(u)
                mm(ps[:, a % 2, 0:P], q[:, 0:P], k[:, 0:P], True, True)
                mm(ps[:, a % 2, P:3 * P], q[:, P:SEQ], k, True, True).then_inc(scores_ready, 1)

            def turn(a):
                pe.wait_ge(exp_done, a + 1)
                if a >= 2:
                    pe.wait_ge(pT_ready, a - 1)
                for b in range(3):
                    last = pe.transpose(ps[:, 2 + a % 2, b * P:(b + 1) * P],
                                        work[:, 2 + a % 2, b * P:(b + 1) * P], ident)
                last.then_inc(probs_turned, 1)

            def values(a, u):
                pe.wait_ge(pT_ready, a + 1)
                if a >= 2:
                    pe.wait_ge(attn_stored, a - 1)
                pT = work[:, 4 + a % 2, :]
                w = P if u["kind"] == "diff" else 64
                o = ps[:, 4 + a % 2, :]
                mm(o[:, 0:w], pT[:, 0:P], unit_v(u, 0), True, True)
                mm(o[:, w:2 * w], pT[:, P:2 * P], unit_v(u, 0), True, False)
                mm(o[:, w:2 * w], pT[:, 2 * P:3 * P], unit_v(u, 1), False, True).then_inc(attn_out, 1)

            def attention(l):
                for s in range(NU + 2):
                    if s < NU:
                        scores(l * NU + s, UNITS[s])
                    if 1 <= s <= NU:
                        turn(l * NU + s - 1)
                    if s >= 2:
                        values(l * NU + s - 2, UNITS[s - 2])

            def branches_T(l):
                pc = l * PIECES_LAYER + N_PIECES_PROJ + N_PIECES_MLA
                for b in range(4):
                    for fp in range(2):
                        bank = piece_bank(pc)
                        for j in range(2):
                            for tt in range(TT):
                                f = 2 * fp + j
                                last = pe.transpose(bank[:, j * SEQ + tt * P:j * SEQ + tt * P + P],
                                                    yR[:, b, tt, f * P:(f + 1) * P], ident)
                        last.then_inc(piece_ready, 1)
                        pc += 1
                for n in (pc - 1, pc - 2):
                    s, v = piece_copied(n)
                    pe.wait_ge(s, v)

            def merge(l):
                c0 = layer_slot(l) + C_FFN + C_MIX
                for m in range(32):
                    ct, b = m // 4, m % 4
                    c = c0 + m // 2
                    o = (m % 2) * 1536
                    M = 32 * l + m
                    split_weights(c)
                    if M >= 4:
                        pe.wait_ge(merged, M - 3)
                    for k in range(KD):
                        stationary_weights(ps[:, m % 4, 0:SEQ], c, slice(o + k * P, o + (k + 1) * P), k,
                                           k == 0, k == KD - 1)
                    for k in range(4):
                        last = mm(ps[:, m % 4, SEQ:2 * SEQ], slot(c)[:, o + D + k * P:o + D + (k + 1) * P],
                                  yT[:, b, k, :], k == 0, k == 3)
                    last.then_inc(gb_ready, 1)
                    if m % 2:
                        pending[0] += 1
                pe.wait_ge(merged, 32 * (l + 1))
                out_project(c0 + C_GB, lambda k, tt: mT[:, k, tt * P:(tt + 1) * P], KD)

            def out_project(c0, lhs, nk):
                for k in range(nk):
                    c = c0 + k // 3
                    weights(c)
                    for tt in range(TT):
                        for half in range(2):
                            last = mm(ps[:, 4 + tt * 2 + half, :], lhs(k, tt),
                                      slot(c)[:, (k % 3) * D + half * 512:(k % 3) * D + half * 512 + 512],
                                      k == 0, k == nk - 1)
                    if k % 3 == 2 or k == nk - 1:
                        pending[0] += 1
                last.then_inc(wo_ready, 1)

            def piece_bank_2(g):
                s, v = piece_copied(g - 2)
                pe.wait_ge(s, v)
                return ps[:, 6 + g % 2, :]

            def tile_piece(g, c, t):
                bank = piece_bank_2(g)
                for k in range(KD):
                    last = stationary_weights(bank[:, 0:SEQ], c, slice(t * D + k * P, t * D + (k + 1) * P), k,
                                              k == 0, k == KD - 1)
                last.then_inc(piece_ready, 1)

            def row_piece(g, c, tt):
                bank = piece_bank_2(g)
                for k in range(KD):
                    last = moving_weights(bank[:, 0:A_COLS], c, slice(k * A_COLS, (k + 1) * A_COLS), k, tt,
                                          k == 0, k == KD - 1)
                last.then_inc(piece_ready, 1)

            def bias_vectors_2():
                pe.wait_ge(params_2_in, 16 * 3)
                pe.wait_ge(table_2_masked, 1)
                for n, (o, w, g) in enumerate(VEC_2_PARTS):
                    last = pe.matmul(ps[0:16, n, 0:w], table_2_sb[:, 16 * g:16 * g + 16], picks_2[:, o:o + w],
                                     start=True, stop=True)
                last.then_inc(vec_2_ready, 1)

            def dilated_pieces(c0, hp, ns):
                for n in ns:
                    g = PIECES_DIL + 8 * hp + n
                    c = c0 + 3 * hp + (n // 3 if n < 6 else 2)
                    split_weights(c)
                    if n < 6:
                        tile_piece(g, c, n % 3)
                    else:
                        row_piece(g, c, n - 6)
                    if n in (2, 5, 7):
                        pending[0] += 1

            def dilated_scores(d):
                head, qt = d // 2, d % 2
                hp, r = head // 2, slice(64 * (head % 2), 64 * (head % 2) + 64)
                b = hp % 2
                if d % 4 == 0:
                    for g in (PIECES_DIL + 8 * hp + 6, PIECES_DIL + 8 * hp + 7):
                        s, v = piece_copied(g)
                        pe.wait_ge(s, v)
                if qt == 0:
                    pe.wait_ge(hankel_2_in[head % 4], 64 * (head // 4 + 1))
                if d == 0:
                    pe.wait_ge(flip_2_in, 16)
                if d >= 2:
                    pe.wait_ge(exp_2_done, d - 1)
                S = ps[:, d % 2, :]
                x = hankel_2[:, head % 4, :]
                first = 2 * (1 - qt) * 64
                mm(S[:, 0:256], flip_2, x[:, first:first + 256], True, False, skip_group_check=True)
                pe.matmul(S[:, 256:512], flip_2, x[:, 384:640], start=False, stop=False, skip_group_check=True)
                for g in range(N_GROUPS):
                    q = qkD[r, b, 2 * g, qt * P:(qt + 1) * P]
                    k = qkD[r, b, 2 * g + 1, :] if g == 0 else qkD[r, b, 2 * g + 1, qt * P:(qt + 1) * P]
                    o = S[:, 0:256] if g == 0 else S[:, 128 * (g + 1):128 * (g + 2)]
                    last = pe.matmul(o, q, k, start=False, stop=True, skip_group_check=True)
                last.then_inc(scores_2, 1)

            def dilated_turn(d):
                pe.wait_ge(exp_2_done, d + 1)
                if d >= 2:
                    pe.wait_ge(pT_2_ready, d - 1)
                for n in range(4):
                    last = pe.transpose(ps[:, 2 + d % 2, n * P:(n + 1) * P], probs[:, d % 2, n * P:(n + 1) * P], ident)
                last.then_inc(turned_2, 1)

            def dilated_values(d):
                head, qt = d // 2, d % 2
                b, o = (head // 2) % 2, 64 * (head % 2)
                pe.wait_ge(pT_2_ready, d + 1)
                if d >= 2:
                    pe.wait_ge(stored_2, d - 1)
                for n, (g, kt) in enumerate(((0, 0), (0, 1), (1, qt), (2, qt))):
                    last = pe.matmul(ps[:, 4 + d % 2, 0:64], probsT[:, d % 2, n * P:(n + 1) * P],
                                     vD[:, b, kt, g * P + o:g * P + o + 64], start=n == 0, stop=n == 3)
                last.then_inc(out_2, 1)

            def dilated(c0, p):
                pe.wait_ge(uT_dve_ready, KD * (p + 1))
                dilated_pieces(c0, 0, range(8))
                for s in range(NU2 + 2):
                    hp = s // 4 + 1
                    if hp < 8:
                        dilated_pieces(c0, hp, (2 * (s % 4), 2 * (s % 4) + 1))
                    if s < NU2:
                        dilated_scores(s)
                    if 1 <= s <= NU2:
                        dilated_turn(s - 1)
                    if s >= 2:
                        dilated_values(s - 2)
                pe.wait_ge(stored_2, NU2)
                for kp in range(4):
                    g = PIECES_DIL + 64 + kp
                    bank = piece_bank_2(g)
                    for j in range(2):
                        for tt in range(TT):
                            k = 2 * kp + j
                            last = pe.transpose(bank[:, j * SEQ + tt * P:j * SEQ + tt * P + P],
                                                yD[:, tt, k * P:(k + 1) * P], ident)
                    last.then_inc(piece_ready, 1)
                for g in (PIECES_DIL + 66, PIECES_DIL + 67):
                    s, v = piece_copied(g)
                    pe.wait_ge(s, v)
                out_project(c0 + 24, lambda k, tt: mT[:, k, tt * P:(tt + 1) * P], KD)

            def retention(c0, p):
                pe.wait_ge(uT_dve_ready, KD * (p + 1))
                pc = [PIECES_RET]

                def rows_of(hh):
                    for a in range(4):
                        c = c0 + C_RET_QK + 4 * hh + a
                        split_weights(c)
                        for tt in range(TT):
                            row_piece(pc[0], c, tt)
                            pc[0] += 1
                        pending[0] += 1

                def turn(hh):
                    pe.wait_ge(ret_head, hh + 1)
                    for n in range(2):
                        bank = piece_bank_2(pc[0])
                        for j in range(2):
                            for tt in range(TT):
                                f = 2 * n + j
                                last = pe.transpose(bank[:, j * SEQ + tt * P:j * SEQ + tt * P + P],
                                                    yH[:, tt, f * P:(f + 1) * P], ident)
                        last.then_inc(piece_ready, 1)
                        pc[0] += 1

                for t in range(16):
                    c = c0 + t // 3
                    split_weights(c)
                    tile_piece(pc[0], c, t % 3)
                    pc[0] += 1
                    if t % 3 == 2 or t == 15:
                        pending[0] += 1
                rows_of(0)
                for hh in range(RH):
                    pe.wait_ge(ret_rotated, hh + 1)
                    if hh:
                        pe.wait_ge(ret_inner, hh)
                    for jt in range(TT):
                        for kk in range(2):
                            last = mm(ps[:, 0, jt * SEQ:(jt + 1) * SEQ], qkT[:, 4 * hh + 2 + kk, jt * P:(jt + 1) * P],
                                      qkT[:, 4 * hh + kk, :], kk == 0, kk == 1)
                    last.then_inc(ret_scores, 1)
                    if hh + 1 < RH:
                        rows_of(hh + 1)
                    if hh:
                        turn(hh - 1)
                    for g in (-1, -2):
                        n = PIECES_RET + RET_PIECES.index(("row", hh, 7)) + 1 + g
                        s, v = piece_copied(n)
                        pe.wait_ge(s, v)
                    pe.wait_ge(ret_inner, hh + 1)
                    for d in range(2):
                        for it in range(TT):
                            js = [j for j in range(TT) if (j <= it if d == 0 else j >= it)]
                            for j in js:
                                last = mm(ps[:, 1 + 2 * d + it, :], inner[:, d, j, it * P:(it + 1) * P],
                                          vH[hh % 2][:, j, :], j == js[0], j == js[-1])
                    last.then_inc(ret_y, 1)
                turn(RH - 1)
                for g in (pc[0] - 1, pc[0] - 2):
                    s, v = piece_copied(g)
                    pe.wait_ge(s, v)
                out_project(c0 + C_RET_QK + C_RET_V, lambda k, tt: yT_2[:, k, tt * P:(tt + 1) * P], 16)

            pe.wait_ge(picks_in, 3 * 16)
            pe.wait_ge(table_masked, 1)
            pe.wait_ge(filled, 2)
            pe.matmul(ps[0:8, 0, :], table_sb[:, 0:8], picks_sb[0:33, 0:512], start=True, stop=True)
            pe.matmul(ps[0:13, 1, :], table_sb[:, 8:21], picks_sb[0:33, 512:1024], start=True, stop=True).then_inc(vec_ready, 1)
            pe.wait_ge(params_in, PARAM_DMAS * 16)
            pe.wait_ge(hankel_in, 32)
            pe.wait_ge(vec_copied, 1)
            for n, (_, w) in enumerate(bias_parts()):
                if n >= 8:
                    pe.wait_ge(bias_ready, n - 7)
                src = hankel[n // 8][:, (n % 8) * 512:(n % 8) * 512 + w]
                pe.matmul(ps[:, n % 8, 0:w], flip, src, start=True, stop=True).then_inc(bias_psum, 1)
            end_stage()
            for l in range(DEPTH):
                norm(3 * l)
                ffn(2 * l, layer_slot(l), 3 * l)
                end_stage()
                norm(3 * l + 1)
                projections(l, 3 * l + 1)
                end_stage()
                mla(l)
                end_stage()
                compress(l)
                end_stage()
                attention(l)
                end_stage()
                branches_T(l)
                merge(l)
                end_stage()
                norm(3 * l + 2)
                ffn(2 * l + 1, layer_slot(l) + C_FFN + C_MIX + C_GB + C_WO, 3 * l + 2)
                end_stage()
            bias_vectors_2()
            end_stage()
            for i in range(DEPTH):
                c0 = layer_slot_2(i)
                norm(6 + 3 * i)
                ffn(4 + 2 * i, c0, 6 + 3 * i)
                end_stage()
                norm(7 + 3 * i)
                (dilated if i == 0 else retention)(c0 + C_FFN, 7 + 3 * i)
                end_stage()
                norm(8 + 3 * i)
                ffn(5 + 2 * i, c0 + C_FFN + MIX_2[i], 8 + 3 * i)
                end_stage()

        @block.scalar
        def _(act):
            stage = [0]
            chain = [0]

            def link(ins):
                chain[0] += 1
                ins.then_inc(act_chain, 1)
                act.wait_ge(act_chain, chain[0])

            def end_stage():
                boundary(act, stage[0])
                stage[0] += 1

            def take_high(c, first=False):
                act.wait_ge(weights_in[c % NS], 16 * (c // NS + 1))
                if not first:
                    act.wait_ge(ring_used, SPLIT_SLOTS[SPLIT_INDEX[c] - 2] + 1)
                act.activation(split_part(c, high(c)), split_part(c, ring[:, c % NS, :]), ACT.Copy)\
                    .then_inc(hi_ready, 1)

            def norm(n, p, gain, c0, residues=False):
                squares(n)
                take_high(c0, True)
                act.wait_ge(inv_root_ready, n + 1)
                act.activation(xn[:, 1, :], h[:, 1, :], ACT.Copy, scale=rsq[:, 1:2]).then_inc(xn_act_ready, 1)
                take_high(c0 + 1, True)
                for k in range(KD):
                    act.wait_ge(xT_ready, 4 * p + k // 2 + 1)
                    dst, src = turned_places(uTh, k, ps[:, 4 + k // 2, (k % 2) * SEQ:(k % 2 + 1) * SEQ], residues)
                    act.activation(dst, src, ACT.Copy, scale=gain[:, k:k + 1]).then_inc(uT_act_ready, 1)

            def squares(n):
                for tt in range(TT):
                    act.activation(xn[:, tt, :], h[:, tt, :], ACT.Square,
                                   accum_out=ssq[:, tt:tt + 1]).then_inc(squares_ready, 1)

            def ffn(f, c0):
                def tile(g, i=None):
                    def later(v):
                        return v if i is None else NS * i + v
                    v, c = FT * f + g + 1, c0 + g
                    act.wait_ge(gu_ready, later(v))
                    act.activation(sil[:, g % 2, :], ps[:, 4 + g % 2, 0:SEQ], ACT.Silu).then_inc(silu_ready, 1)
                    if g >= 2:
                        act.wait_ge(ring_used, later(c - 1))
                    act.activation(high(c)[:, 2 * D:3 * D], ring[:, c % NS, 2 * D:3 * D], ACT.Copy)
                    act.wait_ge(prod_ready, later(v))
                    act.activation(hid_hi[:, g % 2, :], prod[:, g % 2, :], ACT.Copy).then_inc(hid_hi_ready, 1)
                    if g + 2 < FT:
                        c += 2
                        w = 16 * (c // NS + 1)
                        act.wait_ge(weights_in[c % NS], w if i is None else 16 * i + w)
                        act.activation(high(c)[:, 0:2 * D], ring[:, c % NS, 0:2 * D], ACT.Copy).then_inc(hi_ready, 1)
                tile(0)
                tile(1)
                with act.Fori(0, (FT - 6) // NS) as i:
                    for t in range(NS):
                        tile(2 + t, i)
                for g in range(FT - 4, FT):
                    tile(g)

            def squares_psum(n, bank):
                for tt in range(TT):
                    act.activation(xn[:, tt, :], ps[:, bank + 2 * tt:bank + 2 * tt + 2, :].rearrange("p a b -> p (a b)"),
                                   ACT.Square, accum_out=ssq[:, tt:tt + 1]).then_inc(squares_ready, 1)

            def copy_2(g, where):
                if g % 2:
                    return
                act.wait_ge(piece_ready, g + 1)
                dst, src, factor = where(g)
                if dst is None:
                    for dst, part in retention_row_parts(*src, factor):
                        last = act.activation(dst, part, ACT.Copy)
                elif factor is None:
                    last = act.activation(dst, src, ACT.Copy)
                else:
                    last = act.activation(dst, src, ACT.Copy, scale=factor)
                last.then_inc(piece_act_out, 1)

            def dilated():
                for n in range(8):
                    copy_2(PIECES_DIL + n, dilated_copy)
                    done_dilated(n, take_high)
                for d in range(NU2):
                    if d // 4 + 1 < 8:
                        for n in (2 * (d % 4), 2 * (d % 4) + 1):
                            copy_2(PIECES_DIL + 8 * (d // 4 + 1) + n, dilated_copy)
                            done_dilated(8 * (d // 4 + 1) + n, take_high)
                    act.wait_ge(max_2_ready, d + 1)
                    if d >= 2:
                        act.wait_ge(turned_2, d - 1)
                    s = small[:, d % 4, :]
                    act.activation(probs[:, d % 2, :], ps[:, d % 2, :], ACT.Exp, bias=s[:, 2:3],
                                   accum_out=s[:, 4:5]).then_inc(exp_2_done, 1)
                for n in range(4):
                    copy_2(PIECES_DIL + 64 + n, dilated_turn_copy)

            def retention():
                at_piece = [PIECES_RET]

                def copies(n):
                    for _ in range(n):
                        copy_2(at_piece[0], retention_copy)
                        done_retention(at_piece[0], take_high)
                        at_piece[0] += 1

                def decay(hh):
                    if hh:
                        act.wait_ge(ret_inner, hh)
                    for d in range(2):
                        last = act.activation(decays[:, d, :], rel[:, d, :], ACT.Exp,
                                              scale=lg[:, 4, 4 * d + hh:4 * d + hh + 1])
                    last.then_inc(ret_exp, 1)

                def swishes(hh):
                    s, v = piece_copied(PIECES_RET + RET_PIECES.index(("row", hh, 0)) + 7)
                    act.wait_ge(s, v)
                    s, v = piece_copied(PIECES_RET + RET_PIECES.index(("row", hh, 0)) + 6)
                    act.wait_ge(s, v)
                    act.activation(swish[hh % 2][:, :, :], swish[hh % 2][:, :, :], ACT.Silu).then_inc(ret_swish, 1)

                act.wait_ge(ret_const_in, 16)
                act.wait_ge(decay_ready, 1)
                copies(16)
                decay(0)
                copies(8)
                swishes(0)
                for hh in range(RH):
                    if hh:
                        act.wait_ge(ret_head, hh)
                    if hh + 1 < RH:
                        copies(8)
                        swishes(hh + 1)
                    if hh:
                        copies(2)
                    if hh + 1 < RH:
                        decay(hh + 1)
                copies(2)

            def copy_pieces(l, first, count, where, splits=False):
                for n in range(count):
                    g = l * PIECES_LAYER + first + n
                    if g % 2 == 0:
                        dst, src = where(n, g)
                        act.wait_ge(piece_ready, g + 1)
                        act.activation(dst, src, ACT.Copy).then_inc(piece_act_out, 1)
                    if splits:
                        done_projection(l, n, take_high)

            def mla(l):
                for tt in range(TT):
                    for j, (o, w) in enumerate(((0, 256), (256, 128))):
                        last = act.activation(xn[:, tt, o:o + w], row[:, tt, o:o + w], ACT.Square,
                                              accum_out=ssq[:, 2 * j + tt:2 * j + tt + 1])
                last.then_inc(mla_squares, 1)
                act.activation(gates[:, :, :], row[:, :, ROW["gate"]:ROW["gate"] + 24],
                               ACT.Sigmoid).then_inc(gates_ready, 1)

            def compress(l):
                act.wait_ge(cmp_hidden, l + 1)
                act.activation(hidC[:, :, :], ps[:, 6:8, 0:2 * NC], ACT.Gelu_apprx_tanh).then_inc(cmp_gelu, 1)
                act.wait_ge(cmp_shifted, l + 1)
                act.activation(ce[:, :, :, :], cs[:, :, :, :], ACT.Exp).then_inc(cmp_exp, 1)

            def exps(a, u, l):
                act.wait_ge(negmax_ready, a + 1)
                if a >= 2:
                    act.wait_ge(probs_turned, a - 1)
                s = small[:, a % 4, :]
                act.activation(work[:, 2 + a % 2, 0:P], work[:, a % 2, 0:P], ACT.Exp,
                               bias=s[:, 2:3], accum_out=s[:, 4:5])
                last = act.activation(work[:, 2 + a % 2, P:3 * P], work[:, a % 2, P:3 * P], ACT.Exp,
                                      bias=s[:, 3:4], accum_out=s[:, 5:6])
                if u["kind"] == "swa":
                    last = act.activation(s[:, 6:8], s[:, 2:4], ACT.Exp, bias=sink[:, l, u["head"]:u["head"] + 1])
                last.then_inc(exp_done, 1)

            def copy_pT(a):
                act.wait_ge(probs_turned, a + 1)
                if a >= 2:
                    act.wait_ge(attn_out, a - 1)
                act.activation(work[:, 4 + a % 2, 0:3 * P], ps[:, 2 + a % 2, 0:3 * P], ACT.Copy).then_inc(pT_ready, 1)

            def attention(l):
                for s in range(NU + 1):
                    if s < NU:
                        exps(l * NU + s, UNITS[s], l)
                    if s >= 1:
                        copy_pT(l * NU + s - 1)

            def merge(l):
                for m in range(32):
                    M = 32 * l + m
                    act.wait_ge(gb_ready, M + 1)
                    if M >= 2:
                        act.wait_ge(merged, M - 1)
                    act.activation(work[:, m % 2, 0:SEQ], ps[:, m % 4, 0:SEQ], ACT.Sigmoid).then_inc(sig_ready, 1)
                    if m % 2:
                        split_after(merge_slot(l) + m // 2, take_high, merge_slot(l) + C_GB)

            for l in range(DEPTH):
                act.wait_ge(lam_sums, l + 1)
                act.activation(nlam[:, l, 0:2], nlam[:, l, 2:4], ACT.Exp).then_inc(lam_exps, 1)
            end_stage()
            for l in range(DEPTH):
                norm(3 * l + 0, 3 * l + 0, norm_g[:, l, 0, :], layer_slot(l))
                ffn(2 * l, layer_slot(l))
                end_stage()
                norm(3 * l + 1, 3 * l + 1, norm_g[:, l, 1, :], layer_slot(l) + C_FFN)
                copy_pieces(l, 0, N_PIECES_PROJ, proj_copies, True)
                end_stage()
                mla(l)
                copy_pieces(l, N_PIECES_PROJ, N_PIECES_MLA, mla_copies)
                end_stage()
                compress(l)
                end_stage()
                attention(l)
                end_stage()
                for j in range(2):
                    take_high(merge_slot(l) + j, True)
                copy_pieces(l, N_PIECES_PROJ + N_PIECES_MLA, 8, branch_copies)
                merge(l)
                end_stage()
                norm(3 * l + 2, 3 * l + 2, norm_g[:, l, 2, :], layer_slot(l + 1) - C_FFN)
                ffn(2 * l + 1, layer_slot(l + 1) - C_FFN)
                end_stage()
            squares(6)
            act.wait_ge(params_2_in, 16 * 3)
            act.activation(lg[:, 1, :], lg[:, 0, :], ACT.Exp).then_inc(decay_exp, 1)
            act.wait_ge(decay_one_minus, 1)
            act.activation(lg[:, 3, :], lg[:, 2, :], ACT.Ln).then_inc(decay_ln, 1)
            end_stage()
            for i in range(DEPTH):
                norm(7 + 6 * i, 6 + 3 * i, norm_g2[:, i, 0, :], layer_slot_2(i))
                ffn(4 + 2 * i, layer_slot_2(i))
                act.wait_ge(ring_used, layer_slot_2(i) + C_FFN)
                squares_psum(8 + 6 * i, 0)
                end_stage()
                norm(9 + 6 * i, 7 + 3 * i, norm_g2[:, i, 1, :], layer_slot_2(i) + C_FFN, residues=i == 0)
                (dilated if i == 0 else retention)()
                act.wait_ge(wo_ready, DEPTH + i + 1)
                squares_psum(10 + 6 * i, 4)
                end_stage()
                norm(11 + 6 * i, 8 + 3 * i, norm_g2[:, i, 2, :], layer_slot_2(i) + C_FFN + MIX_2[i])
                ffn(5 + 2 * i, layer_slot_2(i) + C_FFN + MIX_2[i])
                act.wait_ge(ring_used, layer_slot_2(i) + 2 * C_FFN + MIX_2[i])
                squares_psum(12 + 6 * i, 0)
                end_stage()

        @block.vector
        def _(dve):
            stage = [0]
            chain = [0]

            def link(ins):
                chain[0] += 1
                ins.then_inc(dve_chain, 1)
                dve.wait_ge(dve_chain, chain[0])

            def end_stage():
                boundary(dve, stage[0])
                stage[0] += 1

            def take_low(c):
                dve.wait_ge(hi_ready, SPLIT_INDEX[c] + 1)
                dve.tensor_tensor(split_part(c, ring_lo[:, c % NS, :]), split_part(c, ring[:, c % NS, :]),
                                  split_part(c, high(c).bitcast(F32)), ALU.subtract).then_inc(lo_ready, 1)

            def norm(n, p, gain, c0, residues=False):
                dve.wait_ge(squares_ready, 2 * (n + 1))
                dve.tensor_scalar(ssq[:, 0:TT], ssq[:, 0:TT], 1.0 / D, EPS, ALU.mult, ALU.add).then_inc(mean_ready, 1)
                dve.wait_ge(inv_root_ready, n + 1)
                dve.tensor_scalar(xn[:, 0, :], h[:, 0, :], rsq[:, 0:1], None, ALU.mult).then_inc(xn_dve_ready, 1)
                take_low(c0)
                for k in range(KD):
                    dve.wait_ge(uT_act_ready, KD * p + (k // 2) * 2 + 2)
                    dst, src = turned_places(uTl, k, ps[:, 4 + k // 2, (k % 2) * SEQ:(k % 2 + 1) * SEQ], residues)
                    hi = uTh[:, k, :].bitcast(F32)
                    if residues:
                        hi = hi.rearrange("p (r j) -> p j r", r=4)
                    dve.scalar_tensor_tensor(dst, src, gain[:, k:k + 1], hi, ALU.mult,
                                             ALU.subtract).then_inc(uT_dve_ready, 1)
                take_low(c0 + 1)

            def ffn(f, c0):
                def tile(g, i=None):
                    def later(v):
                        return v if i is None else NS * i + v
                    v, c = FT * f + g + 1, c0 + g
                    dve.wait_ge(silu_ready, later(v))
                    dve.tensor_tensor(prod[:, g % 2, :], sil[:, g % 2, :], ps[:, 4 + g % 2, SEQ:2 * SEQ],
                                      ALU.mult).then_inc(prod_ready, 1)
                    dve.wait_ge(hid_hi_ready, later(v))
                    dve.tensor_tensor(hid_lo[:, g % 2, :], prod[:, g % 2, :], hid_hi[:, g % 2, :].bitcast(F32),
                                      ALU.subtract)
                    dve.tensor_tensor(ring_lo[:, c % NS, 2 * D:3 * D], ring[:, c % NS, 2 * D:3 * D],
                                      high(c)[:, 2 * D:3 * D].bitcast(F32), ALU.subtract).then_inc(hidden_ready, 1)
                    if g + 2 < FT:
                        c += 2
                        dve.wait_ge(hi_ready, later(SPLIT_INDEX[c] + 1))
                        dve.tensor_tensor(ring_lo[:, c % NS, 0:2 * D], ring[:, c % NS, 0:2 * D],
                                          high(c)[:, 0:2 * D].bitcast(F32), ALU.subtract).then_inc(lo_ready, 1)
                tile(0)
                tile(1)
                with dve.Fori(0, (FT - 6) // NS) as i:
                    for t in range(NS):
                        tile(2 + t, i)
                for g in range(FT - 4, FT):
                    tile(g)

            def add_ffn(c_end):
                dve.wait_ge(ring_used, c_end)
                for tt in range(TT):
                    dve.scalar_tensor_tensor(h[:, tt, :], ps[:, 2 * tt:2 * tt + 2, :].rearrange("p a b -> p (a b)"),
                                             0.5, h[:, tt, :], ALU.mult, ALU.add)

            def add_normed(n, bank, gain, factor):
                dve.wait_ge(squares_ready, 2 * (n + 1))
                dve.tensor_scalar(ssq[:, 0:TT], ssq[:, 0:TT], 1.0 / D, EPS, ALU.mult, ALU.add).then_inc(mean_ready, 1)
                dve.wait_ge(inv_root_ready, n + 1)
                for tt in range(TT):
                    last = dve.scalar_tensor_tensor(
                        xn[:, tt, :], ps[:, bank + 2 * tt:bank + 2 * tt + 2, :].rearrange("p a b -> p (a b)"),
                        rsq[:, tt:tt + 1], gain, ALU.mult, ALU.mult)
                link(last)
                for tt in range(TT):
                    dve.scalar_tensor_tensor(h[:, tt, :], xn[:, tt, :], factor, h[:, tt, :], ALU.mult, ALU.add)

            def copy_2(g, where):
                if g % 2 == 0:
                    return
                dve.wait_ge(piece_ready, g + 1)
                dst, src, factor = where(g)
                if dst is None:
                    for dst, part in retention_row_parts(*src, factor):
                        last = dve.tensor_copy(dst, part)
                elif factor is None:
                    last = dve.tensor_copy(dst, src)
                else:
                    last = dve.tensor_scalar(dst, src, factor, None, ALU.mult)
                last.then_inc(piece_dve_out, 1)

            def dilated():
                for n in range(8):
                    copy_2(PIECES_DIL + n, dilated_copy)
                    done_dilated(n, take_low)
                for s in range(NU2 + 2):
                    if s // 4 + 1 < 8:
                        for n in (2 * (s % 4), 2 * (s % 4) + 1):
                            copy_2(PIECES_DIL + 8 * (s // 4 + 1) + n, dilated_copy)
                            done_dilated(8 * (s // 4 + 1) + n, take_low)
                    if s < NU2:
                        dve.wait_ge(scores_2, s + 1)
                        dve.tensor_reduce(small[:, s % 4, 2:3], ps[:, s % 2, :], AX_X, ALU.max,
                                          negate=True).then_inc(max_2_ready, 1)
                    if 1 <= s <= NU2:
                        d = s - 1
                        dve.wait_ge(turned_2, d + 1)
                        if d >= 2:
                            dve.wait_ge(out_2, d - 1)
                        dve.tensor_copy(probsT[:, d % 2, :], ps[:, 2 + d % 2, :]).then_inc(pT_2_ready, 1)
                    if s >= 2:
                        d = s - 2
                        head, qt = d // 2, d % 2
                        sm = small[:, d % 4, :]
                        dve.wait_ge(out_2, d + 1)
                        link(dve.reciprocal(sm[:, 8:9], sm[:, 4:5]))
                        dve.tensor_scalar(yD[:, qt, 64 * head:64 * head + 64], ps[:, 4 + d % 2, 0:64],
                                          sm[:, 8:9], None, ALU.mult).then_inc(stored_2, 1)
                for n in range(4):
                    copy_2(PIECES_DIL + 64 + n, dilated_turn_copy)

            def retention():
                at_piece = [PIECES_RET]

                def copies(n):
                    for _ in range(n):
                        copy_2(at_piece[0], retention_copy)
                        done_retention(at_piece[0], take_low)
                        at_piece[0] += 1

                dve.wait_ge(ret_const_in, 16)
                copies(16)
                s, v = piece_copied(PIECES_RET + 14)
                dve.wait_ge(s, v)
                t = [xn_flat[:, 512 * n:512 * n + 512].rearrange("p (a t) -> p a t", a=2) for n in range(4)]
                cos = rcos.rearrange("p (a t) -> p a t", a=1).to_broadcast([P, 2, SEQ])
                sin = rsin.rearrange("p (a t) -> p a t", a=1).to_broadcast([P, 2, SEQ])
                for hh in range(RH):
                    x1, x2 = qkT[:, 4 * hh:4 * hh + 4:2, :], qkT[:, 4 * hh + 1:4 * hh + 4:2, :]
                    dve.tensor_tensor(t[0], x1, cos, ALU.mult)
                    dve.tensor_tensor(t[1], x2, sin, ALU.mult)
                    dve.tensor_tensor(t[2], x1, sin, ALU.mult)
                    link(dve.tensor_tensor(t[3], x2, cos, ALU.mult))
                    dve.tensor_tensor(x1, t[0], t[1], ALU.subtract)
                    dve.tensor_tensor(x2, t[2], t[3], ALU.add).then_inc(ret_rotated, 1)
                    dve.wait_ge(ret_rotated, hh + 1)
                copies(8)
                for hh in range(RH):
                    dve.wait_ge(ret_exp, hh + 1)
                    link(dve.tensor_tensor(decays, decays, rel_ok, ALU.mult))
                    dve.wait_ge(ret_scores, hh + 1)
                    if hh:
                        dve.wait_ge(ret_y, hh)
                    for d in range(2):
                        last = dve.scalar_tensor_tensor(inner[:, d, :, :].rearrange("p t i -> p (t i)"), ps[:, 0, :],
                                                        DK_R ** -0.5, decays[:, d, :], ALU.mult, ALU.mult)
                    last.then_inc(ret_inner, 1)
                    if hh + 1 < RH:
                        copies(8)
                    if hh:
                        copies(2)
                    dve.wait_ge(ret_y, hh + 1)
                    for n in range(4):
                        last = dve.bn_stats(stats[:, n, :], ps[:, 1 + n, :])
                    link(last)
                    for n in range(4):
                        last = dve.bn_aggr(moments[:, n, 0:2], stats[:, n, :])
                    link(last)
                    dve.tensor_scalar(ssq[:, 0:4], moments[:, :, 1], EPS, None, ALU.add).then_inc(ret_moments, 1)
                    dve.wait_ge(ret_inv, hh + 1)
                    dve.wait_ge(ret_swish, hh + 1)
                    for tt in range(TT):
                        for d in range(2):
                            last = dve.scalar_tensor_tensor(tmpH[:, d, :], ps[:, 1 + 2 * d + tt, :],
                                                            moments[:, 2 * d + tt, 0:1],
                                                            swish[hh % 2][:, tt, 512 * d:512 * d + 512],
                                                            ALU.subtract, ALU.mult)
                        link(last)
                        link(dve.tensor_scalar(tmpH[:, 2, :], tmpH[:, 0, :], rsq[:, tt:tt + 1], None, ALU.mult))
                        last = dve.scalar_tensor_tensor(yH[:, tt, :], tmpH[:, 1, :], rsq[:, 2 + tt:3 + tt],
                                                        tmpH[:, 2, :], ALU.mult, ALU.add)
                        if tt == 0:
                            link(last)
                    last.then_inc(ret_head, 1)
                    dve.wait_ge(ret_head, hh + 1)
                copies(2)

            def final_norm(n):
                dve.wait_ge(squares_ready, 2 * (n + 1))
                dve.tensor_scalar(ssq[:, 0:TT], ssq[:, 0:TT], 1.0 / D, EPS, ALU.mult, ALU.add).then_inc(mean_ready, 1)
                dve.wait_ge(inv_root_ready, n + 1)
                dve.wait_ge(gains_in, 16 * 8)
                for tt in range(TT):
                    dve.scalar_tensor_tensor(h[:, tt, :], h[:, tt, :], rsq[:, tt:tt + 1], gain_rows[0],
                                             ALU.mult, ALU.mult)

            def copy_pieces(l, first, count, where, splits=False):
                for n in range(count):
                    g = l * PIECES_LAYER + first + n
                    if g % 2:
                        dst, src = where(n, g)
                        dve.wait_ge(piece_ready, g + 1)
                        dve.tensor_copy(dst, src).then_inc(piece_dve_out, 1)
                    if splits:
                        done_projection(l, n, take_low)

            def rotate(x, dst, heads, tt):
                cos = rope[:, tt, 0:1, :].to_broadcast([P, heads, 16])
                sin = rope[:, tt, 1:2, :].to_broadcast([P, heads, 16])
                x1, x2 = x[:, :, 0:16], x[:, :, 16:32]
                t = [ropet[:, n, 0:heads, :] for n in range(4)]
                dve.tensor_tensor(t[0], x1, cos, ALU.mult)
                dve.tensor_tensor(t[1], x2, sin, ALU.mult)
                dve.tensor_tensor(t[2], x1, sin, ALU.mult)
                link(dve.tensor_tensor(t[3], x2, cos, ALU.mult))
                dve.tensor_tensor(dst[:, :, 0:16], t[0], t[1], ALU.subtract)
                last = dve.tensor_tensor(dst[:, :, 16:32], t[2], t[3], ALU.add)
                link(last)

            def mla(l):
                dve.wait_ge(mla_squares, l + 1)
                dve.tensor_scalar(ssq[:, 0:2], ssq[:, 0:2], 1.0 / 256, EPS, ALU.mult, ALU.add)
                dve.tensor_scalar(ssq[:, 2:4], ssq[:, 2:4], 1.0 / 128, EPS, ALU.mult, ALU.add).then_inc(mla_mean, 1)
                dve.wait_ge(mla_inv, l + 1)
                for tt in range(TT):
                    dve.tensor_scalar(xn_flat[:, tt * 384:tt * 384 + 256], row[:, tt, 0:256],
                                      rsq[:, tt:tt + 1], None, ALU.mult)
                    last = dve.tensor_scalar(xn_flat[:, tt * 384 + 256:tt * 384 + 384], row[:, tt, 256:384],
                                             rsq[:, 2 + tt:3 + tt], None, ALU.mult)
                last.then_inc(mla_normed, 1)
                dve.wait_ge(mla_cT_psum, l + 1)
                for f in range(3):
                    last = dve.tensor_scalar(cT[:, f, :], ps[:, 4 + f, 0:SEQ], mla_g[:, l, f:f + 1], None, ALU.mult)
                last.then_inc(mla_cT, 1)
                for tt in range(TT):
                    rotate(row[:, tt:tt + 1, ROW["krope"]:ROW["krope"] + 32], kr[:, tt:tt + 1, :], 1, tt)
                    dve.tensor_copy(kR[:, tt, :].rearrange("p (h i) -> p h i", h=MLA_H)[:, :, NOPE:QK_M],
                                    kr[:, tt:tt + 1, :].to_broadcast([P, MLA_H, ROPE]))
                copy_pieces(l, N_PIECES_PROJ, 8, mla_copies)
                for n in range(4):
                    s, v = piece_copied(l * PIECES_LAYER + N_PIECES_PROJ + n)
                    dve.wait_ge(s, v)
                for tt in range(TT):
                    q = qR[:, tt, :].rearrange("p (h i) -> p h i", h=MLA_H)[:, :, NOPE:QK_M]
                    rotate(q, q, MLA_H, tt)
                dve.engine_nop().then_inc(mla_roped, 1)
                for n in range(8, N_PIECES_MLA):
                    g = l * PIECES_LAYER + N_PIECES_PROJ + n
                    if g % 2:
                        dst, src = mla_copies(n, g)
                        dve.wait_ge(piece_ready, g + 1)
                        dve.tensor_copy(dst, src).then_inc(piece_dve_out, 1)

            def compress(l):
                kv = qkT[:, T_CMP:T_CMP + 2, :]
                parts = kv.ap[0]
                windows = bass.AP(tensor=kv.tensor, offset=kv.offset,
                                  ap=[parts, [1, CMP_LEN], [SEQ, 2], [CMP_STRIDE, NC]])
                dve.tensor_tensor(blk, windows, pos[:, l, :].rearrange("p (l a b) -> p l a b", a=1, b=1)
                                  .to_broadcast([P, CMP_LEN, 2, NC]), ALU.add).then_inc(blocks_ready, 1)
                dve.wait_ge(cmp_kv, l + 1)
                dve.tensor_copy(cmps[:, 0:2 * NC], ps[:, 4, 0:2 * NC])
                dve.tensor_copy(vc[0:NC, :], ps[0:NC, 5, 0:P]).then_inc(cmp_kv_out, 1)
                dve.wait_ge(cmp_spread, l + 1)
                r = 8 * NC
                spread = ps[0:r, 6, 0:P].rearrange("p (k g d) -> p k g d", k=2, g=1).to_broadcast([r, 2, 4, HD])
                own = head_of_row.rearrange("p (k g d) -> p k g d", k=2, d=1).to_broadcast([r, 2, 4, HD])
                dve.tensor_tensor(vB[0:r, :, :].rearrange("p (k g) d -> p k g d", k=2), spread, own,
                                  ALU.mult).then_inc(cmp_vB, 1)
                dve.wait_ge(cmp_scores, l + 1)
                for kv in range(2):
                    for tt in range(TT):
                        last = dve.scalar_tensor_tensor(
                            cs[:, tt, 4 * kv:4 * kv + 4, :],
                            ps[:, 7 - 2 * kv, tt * 4 * NC:(tt + 1) * 4 * NC].rearrange("p (h c) -> p h c", h=4),
                            HD ** -0.5, cmp_neg[:, tt:tt + 1, :].to_broadcast([P, 4, NC]), ALU.mult, ALU.add)
                link(last)
                cs16 = cs.rearrange("p t h c -> p (t h) c")
                ce16 = ce.rearrange("p t h c -> p (t h) c")
                link(dve.tensor_reduce(cden[:, 0, :], cs16, AX_X, ALU.max))
                dve.tensor_tensor(cs16, cs16, cden[:, 0, :].unsqueeze(2).to_broadcast([P, 16, NC]),
                                  ALU.subtract).then_inc(cmp_shifted, 1)
                dve.wait_ge(cmp_exp, l + 1)
                for tt in range(TT):
                    last = dve.tensor_tensor(ce[:, tt, :, :], ce[:, tt, :, :],
                                             cmp_ok[:, tt:tt + 1, :].to_broadcast([P, 8, NC]), ALU.mult)
                link(last)
                link(dve.tensor_reduce(cden[:, 1, :], ce16, AX_X, ALU.add))
                link(dve.scalar_tensor_tensor(cden[:, 0, :], cden[:, 1, :], 0.0, cden[:, 1, :], ALU.is_equal, ALU.add))
                link(dve.reciprocal(cden[:, 2, :], cden[:, 0, :]))
                dve.wait_ge(gates_ready, l + 1)
                link(dve.tensor_tensor(cden[:, 1, :].rearrange("p (t h) -> p t h", t=TT),
                                       cden[:, 2, :].rearrange("p (t h) -> p t h", t=TT),
                                       gates[:, :, 0:24:3], ALU.mult))
                dve.tensor_tensor(ce16, ce16, cden[:, 1, :].unsqueeze(2).to_broadcast([P, 16, NC]),
                                  ALU.mult).then_inc(cmp_probs, 1)
                dve.wait_ge(cmp_pT_psum, l + 1)
                dve.tensor_copy(pcT[0:r, :], ps[0:r, 4, 0:SEQ]).then_inc(cmp_pT, 1)
                dve.wait_ge(cmp_out, l + 1)
                dve.tensor_copy(yR[:, 2, :, :], ps[:, 5:7, :])

            def bias_max(a, u):
                dve.wait_ge(scores_ready, a + 1)
                if a >= 2:
                    dve.wait_ge(exp_done, a - 1)
                st, s, b = work[:, a % 2, :], small[:, a % 4, :], u["bias"]
                dve.scalar_tensor_tensor(st[:, 0:P], ps[:, a % 2, 0:P], u["scale"], bias[:, b, P:SEQ],
                                         ALU.mult, ALU.add)
                last = dve.scalar_tensor_tensor(st[:, P:3 * P], ps[:, a % 2, P:3 * P], u["scale"], bias[:, b, :],
                                                ALU.mult, ALU.add)
                last.then_inc(biased, 1)
                dve.wait_ge(biased, a + 1)
                dve.tensor_reduce(s[:, 0:1], st[:, 0:P], AX_X, ALU.max)
                link(dve.tensor_reduce(s[:, 1:2], st[:, P:3 * P], AX_X, ALU.max))
                floor = sink[:, l_of(a), u["head"]:u["head"] + 1] if u["kind"] == "swa" else NEG
                dve.tensor_scalar(s[:, 2:4], s[:, 0:2], floor, -1.0, ALU.max, ALU.mult).then_inc(negmax_ready, 1)

            def l_of(a):
                return a // NU

            def store(a, u, l):
                dve.wait_ge(attn_out, a + 1)
                s = small[:, a % 4, :]
                den = s[:, 4:6]
                if u["kind"] == "swa":
                    link(dve.tensor_tensor(s[:, 10:12], den, s[:, 6:8], ALU.add))
                    den = s[:, 10:12]
                link(dve.reciprocal(s[:, 8:10], den))
                c = s[:, 8:10]
                adds = u["kind"] in ("sel", "win") or u.get("map") == 1
                if u["kind"] in ("sel", "win"):
                    g = 3 * u["head"] + (1 if u["kind"] == "sel" else 2)
                    link(dve.tensor_tensor(s[:, 12:14], c, gates[:, :, g], ALU.mult))
                    c = s[:, 12:14]
                elif u.get("map") == 1:
                    link(dve.tensor_scalar(s[:, 12:14], c, nlam[:, l, 2:3], None, ALU.mult))
                    c = s[:, 12:14]
                if adds and a:
                    dve.wait_ge(attn_stored, a)
                w = P if u["kind"] == "diff" else 64
                for qt in range(TT):
                    o, y = ps[:, 4 + a % 2, qt * w:(qt + 1) * w], unit_y(u, qt)
                    if adds:
                        last = dve.scalar_tensor_tensor(y, o, c[:, qt:qt + 1], y, ALU.mult, ALU.add)
                    else:
                        last = dve.tensor_scalar(y, o, c[:, qt:qt + 1], None, ALU.mult)
                last.then_inc(attn_stored, 1)

            def attention(l):
                for s in range(NU + 2):
                    if s < NU:
                        bias_max(l * NU + s, UNITS[s])
                    if s >= 2:
                        store(l * NU + s - 2, UNITS[s - 2], l)
                dve.wait_ge(attn_stored, NU * (l + 1))
                y = yR[:, 3, :, :].rearrange("p t (h d) -> p (t h) d", h=4)
                sq = xn_flat[:, 0:1024].rearrange("p (n d) -> p n d", n=8)
                link(dve.tensor_tensor(sq, y, y, ALU.mult))
                link(dve.tensor_reduce(ssq[:, 0:8], sq, AX_X, ALU.add))
                dve.tensor_scalar(ssq[:, 0:8], ssq[:, 0:8], 1.0 / P, EPS, ALU.mult, ALU.add).then_inc(diff_sq, 1)
                dve.wait_ge(diff_inv, l + 1)
                link(dve.tensor_tensor(y, y, rsq[:, 0:8].unsqueeze(2).to_broadcast([P, 8, P]), ALU.mult))
                dve.scalar_tensor_tensor(y, y, 1.0 - lam_init(l), sub[:, l:l + 1, :].to_broadcast([P, 8, P]),
                                         ALU.mult, ALU.mult)

            def merge(l):
                for m in range(32):
                    ct, b = m // 4, m % 4
                    M = 32 * l + m
                    dve.wait_ge(sig_ready, M + 1)
                    s, o = work[:, m % 2, 0:SEQ], ps[:, m % 4, SEQ:2 * SEQ]
                    if b == 0:
                        dve.tensor_tensor(mT[:, ct, :], s, o, ALU.mult).then_inc(merged, 1)
                    else:
                        t = work[:, 2 + m % 2, 0:SEQ]
                        link(dve.tensor_tensor(t, s, o, ALU.mult))
                        dve.wait_ge(merged, M)
                        dve.tensor_tensor(mT[:, ct, :], mT[:, ct, :], t, ALU.add).then_inc(merged, 1)
                    if m % 2:
                        split_after(merge_slot(l) + m // 2, take_low, merge_slot(l) + C_GB)
                dve.wait_ge(wo_ready, l + 1)
                for tt in range(TT):
                    dve.tensor_tensor(h[:, tt, :], ps[:, 4 + 2 * tt:6 + 2 * tt, :].rearrange("p a b -> p (a b)"),
                                      h[:, tt, :], ALU.add)

            dve.memset(zero_bf[:, :], 0.0).then_inc(filled, 1)
            dve.memset(half_neg[:, :], -0.5).then_inc(filled, 1)
            dve.memset(table_sb[:, 20:21][0:32], 0.0)
            dve.memset(qkT[32:33, 4, 0:21], NEG).then_inc(table_masked, 1)
            dve.wait_ge(vec_ready, 1)
            dve.tensor_copy(vec_sb[0:8, 0:512], ps[0:8, 0, :])
            dve.tensor_copy(vec_sb[0:13, 512:1024], ps[0:13, 1, :]).then_inc(vec_copied, 1)
            dve.wait_ge(params_in, 16 * PARAM_DMAS)
            for l in range(DEPTH):
                for n in range(2):
                    link(dve.tensor_tensor(xn_flat[:, (2 * l + n) * HD:(2 * l + n + 1) * HD], lamb[:, l, 2 * n, :],
                                           lamb[:, l, 2 * n + 1, :], ALU.mult))
                dve.tensor_reduce(nlam[:, l, 2:4], xn_flat[:, 2 * l * HD:(2 * l + 2) * HD].rearrange("p (n d) -> p n d", n=2),
                                  AX_X, ALU.add).then_inc(lam_sums, 1)
            for l in range(DEPTH):
                dve.wait_ge(lam_exps, l + 1)
                dve.scalar_tensor_tensor(nlam[:, l, 2:3], nlam[:, l, 1:2], -lam_init(l), nlam[:, l, 0:1],
                                         ALU.add, ALU.subtract)
            for n, (dst, w) in enumerate(bias_parts()):
                dve.wait_ge(bias_psum, n + 1)
                dve.tensor_copy(dst, ps[:, n % 8, 0:w]).then_inc(bias_ready, 1)
            end_stage()
            for l in range(DEPTH):
                norm(3 * l + 0, 3 * l + 0, norm_g[:, l, 0, :], layer_slot(l))
                ffn(2 * l, layer_slot(l))
                add_ffn(layer_slot(l) + C_FFN)
                end_stage()
                norm(3 * l + 1, 3 * l + 1, norm_g[:, l, 1, :], layer_slot(l) + C_FFN)
                copy_pieces(l, 0, N_PIECES_PROJ, proj_copies, True)
                end_stage()
                mla(l)
                end_stage()
                compress(l)
                end_stage()
                attention(l)
                end_stage()
                for j in range(2):
                    take_low(merge_slot(l) + j)
                copy_pieces(l, N_PIECES_PROJ + N_PIECES_MLA, 8, branch_copies)
                merge(l)
                end_stage()
                norm(3 * l + 2, 3 * l + 2, norm_g[:, l, 2, :], layer_slot(l + 1) - C_FFN)
                ffn(2 * l + 1, layer_slot(l + 1) - C_FFN)
                add_ffn(layer_slot(l + 1))
                end_stage()
            dve.memset(flatM[32:33, NV_2:NV_2 + 48], NEG).then_inc(table_2_masked, 1)
            final_norm(6)
            dve.wait_ge(decay_exp, 1)
            link(dve.tensor_scalar(lg[:, 2, :], lg[:, 1, :], -1.0, 1.0, ALU.mult, ALU.add))
            dve.tensor_scalar(lg[:, 4, :], lg[:, 2, :], -1.0, 1.0, ALU.mult, ALU.add).then_inc(decay_one_minus, 1)
            dve.wait_ge(decay_one_minus, 1)
            link(dve.tensor_scalar(lg[:, 0, :], lg[:, 4, :], 1e-30, None, ALU.max))
            link(dve.reciprocal(lg[:, 4, :], lg[:, 0, :]))
            link(dve.tensor_tensor(lg[:, 0, :], lg[:, 4, :], lg[:, 1, :], ALU.mult))
            dve.wait_ge(decay_ln, 1)
            dve.tensor_tensor(lg[:, 4, :], lg[:, 0, :], lg[:, 3, :], ALU.mult).then_inc(decay_ready, 1)
            dve.wait_ge(vec_2_ready, 1)
            for n, (o, w, _) in enumerate(VEC_2_PARTS):
                last = dve.tensor_copy(vec_2_sb[:, o:o + w], ps[0:16, n, 0:w])
            last.then_inc(vec_2_copied, 1)
            end_stage()
            for i in range(DEPTH):
                norm(7 + 6 * i, 6 + 3 * i, norm_g2[:, i, 0, :], layer_slot_2(i))
                ffn(4 + 2 * i, layer_slot_2(i))
                add_normed(8 + 6 * i, 0, gain_rows[1 + 3 * i], 0.5)
                end_stage()
                norm(9 + 6 * i, 7 + 3 * i, norm_g2[:, i, 1, :], layer_slot_2(i) + C_FFN, residues=i == 0)
                (dilated if i == 0 else retention)()
                add_normed(10 + 6 * i, 4, gain_rows[2 + 3 * i], 1.0)
                end_stage()
                norm(11 + 6 * i, 8 + 3 * i, norm_g2[:, i, 2, :], layer_slot_2(i) + C_FFN + MIX_2[i])
                ffn(5 + 2 * i, layer_slot_2(i) + C_FFN + MIX_2[i])
                add_normed(12 + 6 * i, 0, gain_rows[3 + 3 * i], 0.5)
                end_stage()

        @block.gpsimd
        def _(pool):
            stage = [0]

            def end_stage():
                boundary(pool, stage[0])
                stage[0] += 1

            def inv_root(n_cols, needs, count, signals):
                pool.wait_ge(needs, count)
                pool.tensor_tensor(rsq[:, 0:n_cols], ssq[:, 0:n_cols], half_neg[:, 0:n_cols],
                                   ALU.pow).then_inc(signals, 1)

            o = 0
            loads = [(h[:, :, :], x_rows), (cst[:, :], consts), (norm_g[:, :, :, :], norm_gT), (mla_g[:, :, :], mla_gT),
                     (flip, flip_dram), (sink[:, :, :], sinks.partition_broadcast(P)), (pos[:, :, :], posT),
                     (lamb[:, :, :, :], lam.partition_broadcast(P)), (sub[:, :, :], subln.partition_broadcast(P))]
            assert len(loads) == PARAM_DMAS
            for dst, src in loads:
                pool.dma_start(dst, src).then_inc(params_in, 16)
            pool.wait_ge(vec_copied, 1)
            pool.dma_start(vecs[0:8, :], vec_sb[0:8, 0:512]).then_inc(vec_stored, 16)
            pool.dma_start(vecs[8:21, :], vec_sb[0:13, 512:1024]).then_inc(vec_stored, 16)
            pool.wait_ge(vec_stored, 32)
            pool.wait_ge(params_in, 16 * PARAM_DMAS)
            for n, (first, count) in enumerate(((0, 16), (16, 5))):
                pool.dma_start(hankel[n][:, 0:count * SEQ].rearrange("p (h k) -> p h k", k=SEQ),
                               bass.AP(tensor=vecs.tensor, offset=first * 512,
                                       ap=[[1, P], [512, count], [1, SEQ]])).then_inc(hankel_in, 16)
            pool.wait_ge(hankel_in, 32)
            end_stage()
            for l in range(DEPTH):
                inv_root(TT, mean_ready, 3 * l + 1, inv_root_ready)
                end_stage()
                inv_root(TT, mean_ready, 3 * l + 2, inv_root_ready)
                end_stage()
                inv_root(4, mla_mean, l + 1, mla_inv)
                end_stage()
                end_stage()
                inv_root(8, diff_sq, l + 1, diff_inv)
                end_stage()
                end_stage()
                inv_root(TT, mean_ready, 3 * l + 3, inv_root_ready)
                end_stage()
            pool.dma_start(table_2_sb[0:32, :], table_2).then_inc(params_2_in, 16)
            pool.dma_start(picks_2, pick_2).then_inc(params_2_in, 16)
            pool.dma_start(lg[:, 0, :], decay.partition_broadcast(P)).then_inc(params_2_in, 16)
            for n in range(7):
                pool.dma_start(gain_rows[n], gains_2[n:n + 1, :].partition_broadcast(P)
                               .rearrange("p a d -> p (a d)")).then_inc(gains_in, 16)
            pool.dma_start(norm_g2[:, :, :, :], norm_gT_2).then_inc(gains_in, 16)
            inv_root(TT, mean_ready, 7, inv_root_ready)
            pool.wait_ge(gains_in, 16 * 8)
            pool.wait_ge(vec_2_copied, 1)
            pool.dma_start(vecs_2, vec_2_sb).then_inc(vec_2_stored, 16)
            pool.dma_start(flip_2, flip_dram).then_inc(flip_2_in, 16)
            pool.wait_ge(vec_2_stored, 16)
            end_stage()

            def load_hankel(head):
                if head >= 4:
                    pool.wait_ge(scores_2, 2 * (head - 3))
                for a in range(2):
                    dst = hankel_2[64 * a:64 * a + 64, head % 4, :]
                    o = head * NV_2 + a * P + 1
                    pool.dma_start(dst[:, 0:384].rearrange("p (c j) -> p c j", j=64),
                                   bass.AP(tensor=vecs_2.tensor, offset=o, ap=[[1, 64], [P, 6], [1, 64]]))\
                        .then_inc(hankel_2_in[head % 4], 16)
                    pool.dma_start(dst[:, 384:640].rearrange("p (c j) -> p c j", j=64),
                                   bass.AP(tensor=vecs_2.tensor, offset=o + 7 * P, ap=[[1, 64], [P, 4], [1, 64]]))\
                        .then_inc(hankel_2_in[head % 4], 16)

            for i in range(DEPTH):
                if i == 1:
                    pool.dma_start(flatR[:, 0:2560], ret_const).then_inc(ret_const_in, 16)
                inv_root(TT, mean_ready, 8 + 6 * i, inv_root_ready)
                if i == 0:
                    for head in range(4):
                        load_hankel(head)
                inv_root(TT, mean_ready, 9 + 6 * i, inv_root_ready)
                end_stage()
                inv_root(TT, mean_ready, 10 + 6 * i, inv_root_ready)
                if i == 0:
                    for head in range(4, HEADS_2):
                        load_hankel(head)
                else:
                    for hh in range(RH):
                        inv_root(4, ret_moments, hh + 1, ret_inv)
                inv_root(TT, mean_ready, 11 + 6 * i, inv_root_ready)
                end_stage()
                inv_root(TT, mean_ready, 12 + 6 * i, inv_root_ready)
                inv_root(TT, mean_ready, 13 + 6 * i, inv_root_ready)
                end_stage()
            for tt in range(TT):
                pool.dma_start(out[tt * P:(tt + 1) * P, :], h[:, tt, :]).then_inc(x_stored, 16)
            pool.wait_ge(x_stored, 32)


def lam_init(l):
    return 0.8 - 0.6 * math.exp(-0.3 * l)



def _tiles(w):
    k, n = w.shape
    return w.reshape(k // P, P, n // P, P).transpose(2, 1, 0, 3)


def pack_stream(x):
    out = np.zeros((N_SLOTS, P, SLOT), np.float32)
    c = 0

    def put(o, a):
        a = a.reshape(P, -1)
        out[c, :, o:o + a.shape[1]] = a

    def ffn(wg, wu, wd):
        nonlocal c
        for part, w in enumerate((wg, wu)):
            out[c:c + FT, :, part * D:(part + 1) * D] = _tiles(w).reshape(FT, P, D)
        out[c:c + FT, :, 2 * D:] = wd.reshape(FT, P, D)
        c += FT

    def rows(w, k_per_slot=3):
        nonlocal c
        t = w.reshape(-1, P, D)
        for k0 in range(0, t.shape[0], k_per_slot):
            for k in range(k0, min(k0 + k_per_slot, t.shape[0])):
                put((k - k0) * D, t[k])
            c += 1

    def turned(w):
        nonlocal c
        t = _tiles(w)
        for n in range(t.shape[0]):
            put((n % T_PER_SLOT) * D, t[n])
            if n % T_PER_SLOT == T_PER_SLOT - 1 or n == t.shape[0] - 1:
                c += 1

    def row_form(w):
        nonlocal c
        for n in range(0, w.shape[1], A_COLS):
            part = w[:, n:n + A_COLS].reshape(KD, P, -1).transpose(1, 0, 2)
            for k in range(KD):
                out[c, :, k * A_COLS:k * A_COLS + part.shape[2]] = part[:, k]
            c += 1

    for l in range(DEPTH):
        ffn(x["ffn_w_gate"][l, 0], x["ffn_w_up"][l, 0], x["ffn_w_down"][l, 0])
        w = {n: x["w_in"][l][:, s:s + z] for (n, s), z in zip(
            _SECT.items(), (256, 128, 32, 512, 128, 128, 512, 128, 128, 128, 128, 128, 128, 24, 512, 512, 512))}
        row_form(np.concatenate([w[n] for n in ROW], 1))

        def paired(q):
            return q.reshape(D, 2, 4, HD).transpose(0, 2, 1, 3).reshape(D, 512)

        cmp_cols = np.concatenate([w["nkc"][:, 0:64], w["nvc"][:, 0:64], w["nkc"][:, 64:], w["nvc"][:, 64:]], 1)
        turned(np.concatenate([paired(w["sq"]), w["sk"], paired(w["nq"]), cmp_cols, w["nks"], w["nkw"],
                               w["dq"], w["dk"]], 1))
        put(0, x["mla_w_uq"][l].reshape(2, P, 768).transpose(1, 0, 2))
        ukv = x["mla_w_ukv"][l].reshape(P, MLA_H, 2, 64).transpose(0, 2, 1, 3)
        put(1536, ukv)
        w2 = x["nsa_cmp_w2"][l]
        put(2560, np.concatenate([w2[0], w2[0], w2[1]], 1))
        c += 1
        w1 = x["nsa_cmp_w1"][l].reshape(2, CMP_LEN, HD, CMP_HID).transpose(0, 2, 1, 3).reshape(P, CMP_LEN, CMP_HID)
        for half in range(2):
            put(0, w1[:, half * 16:(half + 1) * 16])
            c += 1
        wg = np.stack([_tiles(x["w_gate"][l, b]) for b in range(4)], 1)
        wb = np.stack([_tiles(x["w_branch"][l, b]) for b in range(4)], 1)
        for ct in range(KD):
            for b in range(4):
                put((b % 2) * 1536, wg[ct, b])
                put((b % 2) * 1536 + D, wb[ct, b])
                c += b % 2
        rows(x["w_o"][l])
        ffn(x["ffn_w_gate"][l, 1], x["ffn_w_up"][l, 1], x["ffn_w_down"][l, 1])
        assert c == (l + 1) * C_LAYER
    for i in range(DEPTH):
        ffn(x["ffn_w_gate_2"][i, 0], x["ffn_w_up_2"][i, 0], x["ffn_w_down_2"][i, 0])
        if i == 0:
            w = x["attn_w_in_2"][0].reshape(D, N_GROUPS, 3, 8, P)
            for hp in range(8):
                turned(np.concatenate([w[:, g, t, hp] for g in range(N_GROUPS) for t in range(2)], 1))
                row_form(np.concatenate([w[:, g, 2, hp] for g in range(N_GROUPS)], 1))
            rows(x["attn_w_out_2"][0])
        else:
            w = x["ret_w_in_2"][0]
            q, k = (w[:, o:o + 1024].reshape(D, RH, DK_R) for o in (0, 1024))
            turned(np.stack([q, k], 2).reshape(D, 2048))
            v, gf, gb = (w[:, o:o + D_V].reshape(D, RH, DV_R) for o in (2048, 2048 + D_V, 2048 + 2 * D_V))
            for hh in range(RH):
                row_form(np.concatenate([gf[:, hh], gb[:, hh], v[:, hh]], 1))
            rows(x["ret_w_out_2"][0])
        ffn(x["ffn_w_gate_2"][i, 1], x["ffn_w_up_2"][i, 1], x["ffn_w_down_2"][i, 1])
    assert c == N_SLOTS
    return out


def kernel(**inputs):
    import concourse.bacc as bacc
    from concourse.bass_utils import run_bass_kernel_spmd

    x = {k: np.asarray(v) for k, v in inputs.items()}
    c = constants()
    nc = bacc.Bacc("TRN2", target_bir_lowering=False, num_devices=1)
    arrays = {
        "stream": pack_stream(x),
        "x_rows": np.ascontiguousarray(x["x"][0].reshape(TT, P, D).transpose(1, 0, 2)),
        "norm_gT": np.ascontiguousarray(x["norm_g"].reshape(DEPTH, 3, KD, P).transpose(3, 0, 1, 2)),
        "mla_gT": np.ascontiguousarray(np.concatenate([x["mla_q_norm"], x["mla_kv_norm"]], 1)
                                       .reshape(DEPTH, 3, P).transpose(2, 0, 1)),
        "sinks": np.ascontiguousarray(x["swa_sinks"]),
        "posT": np.ascontiguousarray(x["nsa_cmp_pos"].transpose(1, 3, 0, 2).reshape(P, DEPTH, CMP_LEN)),
        "lam": np.ascontiguousarray(x["diff_lambda"]),
        "subln": np.ascontiguousarray(x["diff_subln"]),
        "table_1": np.ascontiguousarray(x["rel_bias_table"]),
        "norm_gT_2": np.ascontiguousarray(x["norm_gains_2"][:, 0::2].reshape(DEPTH, 3, KD, P).transpose(3, 0, 1, 2)),
        "gains_2": np.concatenate([x["final_g"][None], x["norm_gains_2"][:, 1::2].reshape(6, D)], 0),
        "table_2": np.ascontiguousarray(x["rel_bias_2"].T),
        "pick_2": c["pick_2"],
        "ret_const": c["ret_const"],
        "decay": np.ascontiguousarray(x["ret_decay_logit_2"][0].reshape(8)),
        "consts": np.concatenate([c[n] for n in CONST_NAMES], 1),
        "flip_dram": np.ascontiguousarray(np.eye(P, dtype=np.float32)[::-1]),
        "pick_1": np.concatenate([c["pick_window"], c["pick_causal"]], 1),
    }
    args = {n: nc.dram_tensor(n + "_dram", a.shape, mybir.dt.from_np(a.dtype), kind="ExternalInput").ap()
            for n, a in arrays.items()}
    out = nc.dram_tensor("out_dram", (SEQ, D), F32, kind="ExternalOutput").ap()
    build(nc, **args, out=out)
    r = run_bass_kernel_spmd(nc, [{n + "_dram": a for n, a in arrays.items()}], core_ids=[0])
    return r.results[0]["out_dram"].reshape(1, SEQ, D)
```
